# Optimizing a Trainium2 kernel written in Bass

```python
import jax, jax.numpy as jnp
from jax import lax
import numpy as np

D_MODEL = 2048
BATCH = 1
SEQ = 256
DEPTH = 1

D_MIX = D_MODEL
HG_DK = 128
HG_DV = 128
HG_WIDTH = D_MIX // 2
HG_HEADS = HG_WIDTH // HG_DV
HG_QK = HG_HEADS * HG_DK
GDN_DK = 128
GDN_DV = 128
GDN_WIDTH = D_MIX - HG_WIDTH
GDN_HEADS = GDN_WIDTH // GDN_DV
GDN_QK = GDN_HEADS * GDN_DK
CONV_K = 4
CHUNK = 64
D_FF = 4 * D_MODEL
N_MOD = 6
EPS = 1e-6

HG_COLS = 2 * HG_QK + 2 * HG_WIDTH
GDN_CONV_CH = 2 * GDN_QK + GDN_WIDTH
GDN_COLS = GDN_CONV_CH + GDN_WIDTH + 2 * GDN_HEADS
IN_COLS = HG_COLS + GDN_COLS


def rmsnorm(x, w):
    x32 = x.astype(jnp.float32)
    y = x32 * lax.rsqrt(jnp.mean(x32 * x32, axis=-1, keepdims=True) + EPS)
    return (y * w.astype(jnp.float32)).astype(x.dtype)

def l2norm(x):
    return x * lax.rsqrt(jnp.sum(x * x, axis=-1, keepdims=True) + EPS)

def to_chunks(x):
    B, T, H, D = x.shape
    return x.reshape(B, T // CHUNK, CHUNK, H, D).transpose(1, 0, 3, 2, 4)

def from_chunks(x):
    N, B, H, C, D = x.shape
    return x.transpose(1, 0, 3, 2, 4).reshape(B, N * C, H, D)

def causal_conv(u, w):
    ch = u.shape[-1]
    return lax.conv_general_dilated(
        u, w[:, None, :].astype(u.dtype), window_strides=(1,), padding=[(CONV_K - 1, 0)],
        dimension_numbers=('NWC', 'WIO', 'NWC'), feature_group_count=ch)

def hgrn2_chunked(q, log_f, k, v):
    B, T, H, DK = q.shape
    DV = v.shape[-1]
    causal = jnp.tril(jnp.ones((CHUNK, CHUNK), dtype=bool))

    def step(S, xs):
        qc, lfc, kc, vc = xs
        b = jnp.cumsum(lfc, axis=-2)
        diff = b[:, :, :, None, :] - b[:, :, None, :, :]
        decay = jnp.exp(jnp.where(causal[None, None, :, :, None], diff, -jnp.inf))
        attn = jnp.einsum('bhtk,bhsk,bhtsk->bhts', qc, kc, decay)
        o = (jnp.einsum('bhts,bhsv->bhtv', attn, vc)
             + jnp.einsum('bhtk,bhkv->bhtv', qc * jnp.exp(b), S))
        b_last = b[:, :, -1:, :]
        S_new = (S * jnp.exp(b_last[:, :, 0, :, None])
                 + jnp.einsum('bhsk,bhsv->bhkv', kc * jnp.exp(b_last - b), vc))
        return S_new, o

    S0 = jnp.zeros((B, H, DK, DV), jnp.float32)
    _, o = lax.scan(step, S0, (to_chunks(q), to_chunks(log_f), to_chunks(k), to_chunks(v)))
    return from_chunks(o)

def gated_delta_chunked(q, k, v, log_a, beta):
    B, T, H, DK = q.shape
    DV = v.shape[-1]
    qc, kc, vc = to_chunks(q), to_chunks(k), to_chunks(v)
    g = jnp.cumsum(to_chunks(log_a[..., None])[..., 0], axis=-1)
    bc = to_chunks(beta[..., None])[..., 0]
    incl = jnp.tril(jnp.ones((CHUNK, CHUNK), dtype=bool))
    strict = jnp.tril(jnp.ones((CHUNK, CHUNK), dtype=bool), -1)
    gamma = jnp.exp(jnp.where(incl, g[..., :, None] - g[..., None, :], -jnp.inf))
    kk = jnp.einsum('nbhtk,nbhsk->nbhts', kc, kc)
    m = jnp.where(strict, bc[..., :, None] * kk * gamma, 0.0)
    a_mat = jnp.eye(CHUNK, dtype=jnp.float32) + m
    rhs = jnp.concatenate([vc * bc[..., None], kc * (bc * jnp.exp(g))[..., None]], axis=-1)
    sol = lax.linalg.triangular_solve(a_mat, rhs, left_side=True, lower=True, unit_diagonal=True)
    u, w = sol[..., :DV], sol[..., DV:]
    qk = jnp.einsum('nbhtk,nbhsk->nbhts', qc, kc) * gamma
    q_dec = qc * jnp.exp(g)[..., None]
    k_tail = kc * jnp.exp(g[..., -1:] - g)[..., None]
    tail = jnp.exp(g[..., -1])

    def step(S, xs):
        u_c, w_c, qk_c, qd_c, kt_c, tl_c = xs
        v_new = u_c - jnp.einsum('bhck,bhkv->bhcv', w_c, S)
        o = jnp.einsum('bhck,bhkv->bhcv', qd_c, S) + jnp.einsum('bhts,bhsv->bhtv', qk_c, v_new)
        S = S * tl_c[..., None, None] + jnp.einsum('bhck,bhcv->bhkv', kt_c, v_new)
        return S, o

    S0 = jnp.zeros((B, H, DK, DV), jnp.float32)
    _, o = lax.scan(step, S0, (u, w, qk, q_dec, k_tail, tail))
    return from_chunks(o)

def hgrn2_group(p, lb, norm_w):
    B, T, _ = p.shape
    dt = p.dtype
    p32 = p.astype(jnp.float32)
    q = p32[..., :HG_QK].reshape(B, T, HG_HEADS, HG_DK)
    f_logit = p32[..., HG_QK:2 * HG_QK].reshape(B, T, HG_HEADS, HG_DK)
    i_in = p32[..., 2 * HG_QK:2 * HG_QK + HG_WIDTH].reshape(B, T, HG_HEADS, HG_DV)
    g_out = p[..., 2 * HG_QK + HG_WIDTH:].reshape(B, T, HG_HEADS, HG_DV)
    f = lb + (1.0 - lb) * jax.nn.sigmoid(f_logit)
    o = hgrn2_chunked(q, jnp.log(f), 1.0 - f, i_in).astype(dt)
    o = rmsnorm(o, norm_w) * jax.nn.silu(g_out)
    return o.reshape(B, T, HG_WIDTH)

def gdn_group(p, conv_w, a_log, dt_bias, norm_w):
    B, T, _ = p.shape
    dt = p.dtype
    qkv = jax.nn.silu(causal_conv(p[..., :GDN_CONV_CH], conv_w)).astype(jnp.float32)
    q = l2norm(qkv[..., :GDN_QK].reshape(B, T, GDN_HEADS, GDN_DK)) * (GDN_DK ** -0.5)
    k = l2norm(qkv[..., GDN_QK:2 * GDN_QK].reshape(B, T, GDN_HEADS, GDN_DK))
    v = qkv[..., 2 * GDN_QK:].reshape(B, T, GDN_HEADS, GDN_DV)
    off = GDN_CONV_CH
    g_out = p[..., off:off + GDN_WIDTH].reshape(B, T, GDN_HEADS, GDN_DV)
    a = p[..., off + GDN_WIDTH:off + GDN_WIDTH + GDN_HEADS].astype(jnp.float32)
    b = p[..., off + GDN_WIDTH + GDN_HEADS:].astype(jnp.float32)
    log_a = -jnp.exp(a_log.astype(jnp.float32)) * jax.nn.softplus(a + dt_bias.astype(jnp.float32))
    beta = jax.nn.sigmoid(b)
    o = gated_delta_chunked(q, k, v, log_a, beta).astype(dt)
    o = rmsnorm(o, norm_w) * jax.nn.silu(g_out)
    return o.reshape(B, T, GDN_WIDTH)

def first_inputs(seed: int = 0) -> dict:
    key = jax.random.key(seed)
    ks = jax.random.split(key, 20)
    f32 = jnp.float32
    nrm = lambda k, s, sc: jax.random.normal(k, s, f32) * sc
    gain = lambda k, s: 1.0 + 0.05 * jax.random.normal(k, s, f32)
    dtv = jnp.exp(jax.random.uniform(ks[13], (DEPTH, GDN_HEADS), f32, np.log(1e-3), np.log(1e-1)))
    return {
        "x": nrm(ks[0], (BATCH, SEQ, D_MODEL), 1.0),
        "c": nrm(ks[1], (BATCH, D_MODEL), 1.0),
        "w_ada": nrm(ks[2], (DEPTH, D_MODEL, N_MOD * D_MODEL), 0.5 * D_MODEL ** -0.5),
        "b_ada": nrm(ks[3], (DEPTH, N_MOD * D_MODEL), 0.02),
        "pre_mix_norm": gain(ks[4], (DEPTH, D_MODEL)),
        "post_mix_norm": gain(ks[5], (DEPTH, D_MODEL)),
        "pre_ffn_norm": gain(ks[6], (DEPTH, D_MODEL)),
        "post_ffn_norm": gain(ks[7], (DEPTH, D_MODEL)),
        "w_in": nrm(ks[8], (DEPTH, D_MODEL, IN_COLS), D_MODEL ** -0.5),
        "hg_lb_logits": nrm(ks[9], (DEPTH + 1, HG_HEADS, HG_DK), 0.5),
        "hg_norm": gain(ks[10], (DEPTH, HG_DV)),
        "gdn_conv_w": nrm(ks[11], (DEPTH, CONV_K, GDN_CONV_CH), CONV_K ** -0.5),
        "gdn_a_log": jnp.log(jax.random.uniform(ks[12], (DEPTH, GDN_HEADS), f32, 1.0, 16.0)),
        "gdn_dt_bias": dtv + jnp.log(-jnp.expm1(-dtv)),
        "gdn_norm": gain(ks[14], (DEPTH, GDN_DV)),
        "w_out": nrm(ks[15], (DEPTH, D_MIX, D_MODEL), D_MIX ** -0.5),
        "w_ff1": nrm(ks[16], (DEPTH, D_MODEL, D_FF), D_MODEL ** -0.5),
        "w_ff2": nrm(ks[17], (DEPTH, D_FF, D_MODEL), D_FF ** -0.5),
    }

def first_block(x, c, w_ada, b_ada, pre_mix_norm, post_mix_norm, pre_ffn_norm, post_ffn_norm,
              w_in, hg_lb_logits, hg_norm, gdn_conv_w, gdn_a_log, gdn_dt_bias, gdn_norm,
              w_out, w_ff1, w_ff2):
    lb_all = jnp.cumsum(jax.nn.softmax(hg_lb_logits.astype(jnp.float32), axis=0), axis=0)
    c_act = jax.nn.silu(c)
    for l in range(DEPTH):
        mod = c_act @ w_ada[l] + b_ada[l]
        sh_m, sc_m, gt_m, sh_f, sc_f, gt_f = jnp.split(mod[:, None, :], N_MOD, axis=-1)
        h = rmsnorm(x, pre_mix_norm[l]) * (1.0 + sc_m) + sh_m
        proj = h @ w_in[l]
        o_hg = hgrn2_group(proj[..., :HG_COLS], lb_all[l], hg_norm[l])
        o_gdn = gdn_group(proj[..., HG_COLS:], gdn_conv_w[l], gdn_a_log[l], gdn_dt_bias[l], gdn_norm[l])
        y = jnp.concatenate([o_hg, o_gdn], axis=-1) @ w_out[l]
        x = x + gt_m * rmsnorm(y, post_mix_norm[l])
        h = rmsnorm(x, pre_ffn_norm[l]) * (1.0 + sc_f) + sh_f
        y = jnp.square(jax.nn.relu(h @ w_ff1[l])) @ w_ff2[l]
        x = x + gt_f * rmsnorm(y, post_ffn_norm[l])
    return x


D_CONV = D_MODEL // 2
CONV_WIDTH = 3
N_HEADS = 16
N_KV_HEADS = 4
HEAD_DIM = 64
D_ATTN = N_HEADS * HEAD_DIM
D_KV = N_KV_HEADS * HEAD_DIM
WINDOW = 128
BLOCK = 128
ROPE_THETA = 10000.0
N_BRANCH = 2
D_FF_2 = 5632

SPLIT_SIZES = (D_CONV, D_CONV, D_CONV, D_ATTN, D_KV, D_KV, D_MODEL, D_MODEL)
SPLIT_POINTS = tuple(int(p) for p in np.cumsum(SPLIT_SIZES)[:-1])
D_IN_PROJ = int(sum(SPLIT_SIZES))


def rmsnorm_2(x, g):
    xf = x.astype(jnp.float32)
    y = xf * lax.rsqrt(jnp.mean(xf * xf, axis=-1, keepdims=True) + EPS)
    return (y * g.astype(jnp.float32)).astype(x.dtype)

def centred_dwconv3(x, w):
    xp = jnp.pad(x, ((0, 0), (1, 1), (0, 0)))
    return xp[:, :-2] * w[0] + xp[:, 1:-1] * w[1] + xp[:, 2:] * w[2]

def rope(x, seq_len):
    half = HEAD_DIM // 2
    inv_freq = ROPE_THETA ** (-jnp.arange(0, half, dtype=jnp.float32) / half)
    ang = jnp.arange(seq_len, dtype=jnp.float32)[:, None] * inv_freq[None, :]
    cos = jnp.cos(ang)[None, :, None, :]
    sin = jnp.sin(ang)[None, :, None, :]
    xf = x.astype(jnp.float32)
    x1, x2 = xf[..., :half], xf[..., half:]
    out = jnp.concatenate([x1 * cos - x2 * sin, x2 * cos + x1 * sin], axis=-1)
    return out.astype(x.dtype)

def banded_window_attention(q, k, v, sink):
    b, s = q.shape[0], q.shape[1]
    nb = s // BLOCK
    grp = N_HEADS // N_KV_HEADS
    qb = q.reshape(b, nb, BLOCK, N_KV_HEADS, grp, HEAD_DIM)
    pad = ((0, 0), (BLOCK, BLOCK), (0, 0), (0, 0))
    kp = jnp.pad(k, pad).reshape(b, nb + 2, BLOCK, N_KV_HEADS, HEAD_DIM)
    vp = jnp.pad(v, pad).reshape(b, nb + 2, BLOCK, N_KV_HEADS, HEAD_DIM)
    kb = jnp.concatenate([kp[:, :-2], kp[:, 1:-1], kp[:, 2:]], axis=2)
    vb = jnp.concatenate([vp[:, :-2], vp[:, 1:-1], vp[:, 2:]], axis=2)
    scale = HEAD_DIM ** -0.5
    scores = jnp.einsum('bnqkgd,bnskd->bnkgqs', qb, kb).astype(jnp.float32) * scale
    blk = jnp.arange(nb)[:, None, None]
    qpos = blk * BLOCK + jnp.arange(BLOCK)[None, :, None]
    kpos = (blk - 1) * BLOCK + jnp.arange(3 * BLOCK)[None, None, :]
    mask = (jnp.abs(kpos - qpos) <= WINDOW) & (kpos >= 0) & (kpos < s)
    scores = jnp.where(mask[None, :, None, None], scores, -jnp.inf)
    sk = sink.astype(jnp.float32).reshape(1, 1, N_KV_HEADS, grp, 1)
    m = jnp.maximum(jnp.max(scores, axis=-1), sk)
    p = jnp.exp(scores - m[..., None])
    denom = jnp.sum(p, axis=-1) + jnp.exp(sk - m)
    p = (p / denom[..., None]).astype(v.dtype)
    out = jnp.einsum('bnkgqs,bnskd->bnqkgd', p, vb)
    return out.reshape(b, s, N_HEADS, HEAD_DIM)

def second_inputs(seed: int = 0) -> dict:
    key = jax.random.key(seed)
    ks = jax.random.split(key, 16)
    f32 = jnp.float32

    def nrm(k, shape, fan_in):
        return jax.random.normal(k, shape, f32) * (fan_in ** -0.5)

    x = jax.random.normal(ks[0], (BATCH, SEQ, D_MODEL), f32)
    return {
        "x": x,
        "norm_mix_g": 1.0 + 0.02 * jax.random.normal(ks[1], (DEPTH, D_MODEL), f32),
        "w_in": nrm(ks[2], (DEPTH, D_MODEL, D_IN_PROJ), D_MODEL),
        "b_gate": 0.02 * jax.random.normal(ks[3], (DEPTH, N_BRANCH * D_MODEL), f32),
        "conv_a_w": nrm(ks[4], (DEPTH, CONV_WIDTH, D_CONV), CONV_WIDTH),
        "w_out_a": nrm(ks[5], (DEPTH, D_CONV, D_MODEL), D_CONV),
        "sink_logits": 0.5 * jax.random.normal(ks[6], (DEPTH, N_HEADS), f32),
        "w_o_attn": nrm(ks[7], (DEPTH, D_ATTN, D_MODEL), D_ATTN),
        "w_mix_out": nrm(ks[8], (DEPTH, D_MODEL, D_MODEL), D_MODEL),
        "norm_ffn_g": 1.0 + 0.02 * jax.random.normal(ks[9], (DEPTH, D_MODEL), f32),
        "ffn_w_up": nrm(ks[10], (DEPTH, D_MODEL, 2 * D_FF_2), D_MODEL),
        "ffn_conv_w": nrm(ks[11], (DEPTH, CONV_WIDTH, 2 * D_FF_2), CONV_WIDTH),
        "ffn_conv_b": 0.02 * jax.random.normal(ks[12], (DEPTH, 2 * D_FF_2), f32),
        "ffn_w_down": nrm(ks[13], (DEPTH, D_FF_2, D_MODEL), D_FF_2),
        "norm_final_g": 1.0 + 0.02 * jax.random.normal(ks[14], (D_MODEL,), f32),
    }

def second_block(x, norm_mix_g, w_in, b_gate, conv_a_w, w_out_a, sink_logits, w_o_attn,
              w_mix_out, norm_ffn_g, ffn_w_up, ffn_conv_w, ffn_conv_b, ffn_w_down,
              norm_final_g):
    b, s, _ = x.shape
    h = x
    for l in range(DEPTH):
        u = rmsnorm_2(h, norm_mix_g[l])
        z = u @ w_in[l]
        b_a, c_a, v_a, q, k, v, gl_a, gl_b = jnp.split(z, SPLIT_POINTS, axis=-1)
        y_a = (b_a * centred_dwconv3(c_a * v_a, conv_a_w[l])) @ w_out_a[l]
        q = rope(q.reshape(b, s, N_HEADS, HEAD_DIM), s)
        k = rope(k.reshape(b, s, N_KV_HEADS, HEAD_DIM), s)
        v = v.reshape(b, s, N_KV_HEADS, HEAD_DIM)
        att = banded_window_attention(q, k, v, sink_logits[l])
        y_b = att.reshape(b, s, D_ATTN) @ w_o_attn[l]
        g_a = jax.nn.sigmoid(gl_a + b_gate[l, :D_MODEL])
        g_b = jax.nn.sigmoid(gl_b + b_gate[l, D_MODEL:])
        h = h + (g_a * y_a + g_b * y_b) @ w_mix_out[l]
        u2 = rmsnorm_2(h, norm_ffn_g[l])
        up = centred_dwconv3(u2 @ ffn_w_up[l], ffn_conv_w[l]) + ffn_conv_b[l]
        a, gv = up[..., :D_FF_2], up[..., D_FF_2:]
        h = h + (jax.nn.silu(a) * gv) @ ffn_w_down[l]
    return rmsnorm_2(h, norm_final_g)


def setup_inputs(seed=0):
    out = dict(first_inputs(seed))
    for name, value in second_inputs(seed + 1).items():
        if name != "x":
            out[name + "_2"] = value
    return out


def reference(
    x, c, w_ada, b_ada, pre_mix_norm, post_mix_norm, pre_ffn_norm, post_ffn_norm, w_in,
    hg_lb_logits, hg_norm, gdn_conv_w, gdn_a_log, gdn_dt_bias, gdn_norm, w_out, w_ff1, w_ff2,
    norm_mix_g_2, w_in_2, b_gate_2, conv_a_w_2, w_out_a_2, sink_logits_2, w_o_attn_2,
    w_mix_out_2, norm_ffn_g_2, ffn_w_up_2, ffn_conv_w_2, ffn_conv_b_2, ffn_w_down_2,
    norm_final_g_2,
):
    x = first_block(
        x, c, w_ada, b_ada, pre_mix_norm, post_mix_norm, pre_ffn_norm, post_ffn_norm, w_in,
        hg_lb_logits, hg_norm, gdn_conv_w, gdn_a_log, gdn_dt_bias, gdn_norm, w_out, w_ff1,
        w_ff2,
    )
    return second_block(
        x, norm_mix_g_2, w_in_2, b_gate_2, conv_a_w_2, w_out_a_2, sink_logits_2, w_o_attn_2,
        w_mix_out_2, norm_ffn_g_2, ffn_w_up_2, ffn_conv_w_2, ffn_conv_b_2, ffn_w_down_2,
        norm_final_g_2,
    )


_drawn_inputs = setup_inputs


def setup_inputs(seed=0):
    import zlib

    import numpy as np

    out = dict(_drawn_inputs(seed))
    spreads = {}
    factors = {'post_mix_norm': 2.689,
     'pre_ffn_norm': 2.752,
     'post_ffn_norm': 2.962,
     'hg_norm': 3.445,
     'gdn_norm': 4.327,
     'norm_mix_g_2': 3.163,
     'b_gate_2': 8.0,
     'sink_logits_2': 64.0,
     'norm_ffn_g_2': 15.54,
     'ffn_conv_b_2': 15.13,
     'norm_final_g_2': 7.946}
    for name, (base, spread) in spreads.items():
        noise = np.random.default_rng([zlib.crc32(name.encode()), seed]).standard_normal(out[name].shape)
        drawn = base * np.exp(spread * noise) if base else spread * noise
        out[name] = __import__('jax').numpy.asarray(drawn.astype(out[name].dtype))
    for name, factor in factors.items():
        out[name] = (out[name] * factor).astype(out[name].dtype)
    return out
```

```python
from contextlib import ExitStack

import numpy as np
import concourse.bass as bass
from concourse import mybir

F32 = mybir.dt.float32
F32R = mybir.dt.float32r
U32 = mybir.dt.uint32
ALU = mybir.AluOpType
ACT = mybir.ActivationFunctionType
AX = mybir.AxisListType

P = 128
SEQ = 256
NT = SEQ // P
D = 2048
KT = D // P
CH = 512
PK = 2
RAW = 4
HEADS = 8
GH = 4
GROUPS = HEADS // GH
UN = GH * NT
LEVELS = 7
EPS = 1e-6
LOWEST = -87.0
FF1 = 4 * D
FF2 = 5632
AH, AKV, AD = 16, 4, 64
HG_COLS = 4096
CONV_COLS = 3072

C_ID = 0
C_UP = C_ID + P
C_LEV = C_UP + P
C_COS = C_LEV + LEVELS * P
C_SIN = C_COS + NT * 32
C_MASK = C_SIN + NT * 32
C_END = C_MASK + NT * SEQ

ROW_TILES = [
    [("c", KT), ("pre_mix", KT), ("pre_ffn", KT), ("mix2", KT), ("ffn2", KT), ("lb", 2 * HEADS), ("conv_a", 24)],
    [("gdn_conv", 96)],
    [("ffn_conv0", 88)],
    [("ffn_conv1", 88)],
    [("ffn_conv2", 88)],
    [("ffn_bias", 88)],
    [("b_ada", 96)],
]


def constants():
    t = np.zeros((P, C_END), np.float32)
    i = np.arange(P)
    t[:, C_ID:C_ID + P] = np.eye(P)
    t[:, C_UP:C_UP + P] = i[:, None] <= i[None, :]
    for lev in range(LEVELS):
        h = 1 << lev
        same = i[:, None] // (2 * h) == i[None, :] // (2 * h)
        low = (i[:, None] // h) % 2 == 0
        high = (i[None, :] // h) % 2 == 1
        t[:, C_LEV + lev * P:C_LEV + (lev + 1) * P] = same & low & high
    freq = (np.float32(10000.0) ** (-np.arange(32, dtype=np.float32) / np.float32(32))).astype(np.float32)
    ang = np.arange(SEQ, dtype=np.float32)[:, None] * freq[None, :]
    cos, sin = np.cos(ang).astype(np.float32), np.sin(ang).astype(np.float32)
    k = np.arange(SEQ)
    for n in range(NT):
        t[:, C_COS + 32 * n:C_COS + 32 * n + 32] = cos[n * P:(n + 1) * P]
        t[:, C_SIN + 32 * n:C_SIN + 32 * n + 32] = sin[n * P:(n + 1) * P]
        q = n * P + i
        t[:, C_MASK + SEQ * n:C_MASK + SEQ * (n + 1)] = np.where(np.abs(k[None, :] - q[:, None]) <= 128, 0.0, -1e30)
    return t


SECTIONS = [
    ("ada", 0, 64),
    ("hg", 64, 64),
    ("gdn", 64, 64),
    ("out", 32, 0),
    ("ffn", 256, 0),
    ("in2", 72, 0),
    ("gate", 96, 0),
    ("mix", 32, 0),
    ("ffn2", 264, 0),
]
STREAM, GEMM = {}, {}
_s = _g = 0
for _name, _n, _m in SECTIONS:
    STREAM[_name], GEMM[_name] = _s, _g
    _s, _g = _s + _n + _m, _g + _n

HG_TILES = ["q", "f"] + [f"lev{n}" for n in range(LEVELS)] + ["diag", "kh", "s1", "o", "turn"]
GDN_TILES = (["q", "k", "v", "sq", "sk", "grow", "beta", "kk", "qk", "kt", "vt", "p0"]
             + [f"{x}{n}" for n in range(1, LEVELS) for x in ("p", "xp", "px") if (n, x) != (LEVELS - 1, "xp")]
             + ["u", "wt", "s1", "ws", "o", "turn"])
ATT_TILES = (["cv0", "b0", "cv1", "b1", "kt", "qt0", "qt1", "sc0"]
             + [x for n in range(8) for x in ([f"sc{n + 1}"] if n < 7 else []) + [f"pt{n}", f"pv{n}"]] + ["at0", "at1"])
TILE = {}


def _number(name, tiles, groups=1):
    global _t
    for g in range(groups):
        for k, tile in enumerate(tiles):
            TILE[(name, g, tile)] = _t + k
        _t += len(tiles)


_t = 0
_number("rows", ["rows"])
_number("mod", ["shsc"])
_number("op0", ["t0", "t1", "t2", "t3"])
_number("hg", HG_TILES, GROUPS)
_number("mod2", ["shsc"])
_number("gs", ["g"])
_number("gdn", GDN_TILES, GROUPS)
_number("gt", ["m0", "m1", "f0", "f1"])
_number("op1", ["t0", "t1", "t2", "t3"])
_number("op2", ["t0", "t1", "t2", "t3"])
_number("att", ATT_TILES)
_number("op3", ["t0", "t1", "t2", "t3"])

USES = {}
_u = [0, 0, 0]
for _name, _n in [("hg", (4, 4, 0)), ("gdn", (4, 4, 0)), ("ab", (1, 0, 0)), ("out", (2, 2, 0)), ("ffn", (32, 32, 16)),
                  ("in2", (5, 4, 0)), ("gate", (8, 8, 0)), ("mix", (2, 2, 0)), ("ffn2", (33, 22, 11))]:
    USES[_name] = list(_u)
    _u = [a + b for a, b in zip(_u, _n)]


def two_blocks(nc, ins, consts, out, probe=None):
    a = ins
    with ExitStack() as ctx:
        def sem(name):
            return ctx.enter_context(nc.semaphore(name))

        KB = 1024
        BASE = 16512
        slab = ctx.enter_context(nc.sbuf_tensor("slab", [P, 207 * KB // 4 + 64], F32))

        def at(name, shape, kb, dt=F32):
            n = 4 * int(np.prod(shape))
            assert kb * KB + n <= 207 * KB, (name, kb, n)
            return nc.alloc_sbuf_tensor_at(name, [P] + list(shape), dt, offset=BASE + int(kb * KB))

        raw = at("raw", [RAW, PK, CH], 0)
        w_hi = at("w_hi", [RAW, PK, CH], 16, F32R)
        w_lo = at("w_lo", [RAW, PK, CH], 32, F32R)
        op_a = [at("op_a_hi", [KT, SEQ], 48, F32R), at("op_a_lo", [KT, SEQ], 64, F32R)]
        op_b = [[at(f"op_b{n}{x}", [KT // 2, SEQ], 80 + 16 * n + 8 * k, F32R) for k, x in enumerate(("_hi", "_lo"))]
                for n in range(2)]
        table = at("table", [C_END], 112)
        cols = at("cols", [7, P], 119)
        small = at("small", [256], 122.5)
        head_norm = at("head_norm", [2, P], 123.5)
        ones = at("ones", [P], 124.5)
        X = at("X", [NT, D], 125)
        acc = at("acc", [2, D], 141)
        proj = at("proj", [NT, HG_COLS], 157)
        XN = at("XN", [NT, D], 157)
        H32 = at("H32", [2, 4, SEQ], 173)
        junk = at("junk", [D], 64)
        gate_rows = at("gate_rows", [4, D], 157)
        Y = at("Y", [NT, D], 189)
        rows = at("rows", [7, P], 190)
        ab_raw = at("ab_raw", [KT, 16], 189)
        ab_hi = at("ab_hi", [KT, 16], 190, F32R)
        ab_lo = at("ab_lo", [KT, 16], 191, F32R)
        hg_at = [125, 129, 133, 137, 192, 196, 200, 96, 100, 104, 108]
        hg_t = [at(f"hg_t{n}", [UN, P], k) for n, k in enumerate(hg_at)]
        gd_at = [125, 129, 133, 137, 192, 196, 200] + [48 + 4 * n for n in range(8)]
        gd_t = [at(f"gd_t{n}", [UN, P], k) for n, k in enumerate(gd_at)]
        hid = [at("hid_hi", [4, SEQ], 157, F32R), at("hid_lo", [4, SEQ], 161, F32R)]
        relu = at("relu", [NT, CH], 165)
        proj2 = at("proj2", [NT, 9 * CH], 141)
        at_t = [at(f"at_t{n}", [UN, P], 177 + 4 * n) for n in range(7)]
        op_c = [at("op_c_hi", [KT, SEQ], 141, F32R), at("op_c_lo", [KT, SEQ], 157, F32R)]
        za, zb = at("za", [NT, CH], 173), at("zb", [NT, CH], 177)
        ma = at("ma", [2, NT, CH], 181)
        gbias = at("gbias", [2, D], 189)
        hid2 = [at("hid2_hi", [4, SEQ], 157, F32R), at("hid2_lo", [4, SEQ], 161, F32R)]
        up_a, up_g = at("up_a", [NT, CH], 165), at("up_g", [NT, CH], 169)
        cva, cvg = at("cva", [4, SEQ], 173), at("cvg", [4, SEQ], 177)
        sga = at("sga", [4, SEQ], 181)
        fin_norm = at("fin_norm", [D], 141)

        ident = table[:, C_ID:C_ID + P]
        upper = table[:, C_UP:C_UP + P]

        def level(n):
            return table[:, C_LEV + n * P:C_LEV + (n + 1) * P]

        def col(name):
            for r, tile in enumerate(ROW_TILES):
                k = 0
                for what, n in tile:
                    if what == name:
                        return cols[:, r, k:k + n]
                    k += n
            raise KeyError(name)

        used = [0]

        def tiny(n):
            used[0] += n
            assert used[0] <= 256
            return small[:, used[0] - n:used[0]]

        c_act, scale_m, shift_m, scale_f, shift_f = (tiny(KT) for _ in range(5))
        lb, one_lb, tmp16 = tiny(HEADS), tiny(HEADS), tiny(KT)
        sq_sum, rstd, r_a, r_ms, r_b, r_n = (tiny(NT) for _ in range(6))
        eps = tiny(1)
        hsum, hrstd = tiny(UN), tiny(UN)
        k_mx, k_nm, k_sum, k_es, k_rd = (tiny(8) for _ in range(5))
        gsm = at("gsm", [256], 205)
        ab = gsm[:, 0:32].rearrange("p (t n) -> p t n", t=NT)
        beta = gsm[:, 32:48].rearrange("p (t n) -> p t n", t=NT)
        log_a = gsm[:, 48:64].rearrange("p (t n) -> p t n", t=NT)
        g_cum = gsm[:, 64:80].rearrange("p (t n) -> p t n", t=NT)
        bg = gsm[:, 80:96].rearrange("p (t n) -> p t n", t=NT)
        gs_t1 = gsm[:, 96:112].rearrange("p (t n) -> p t n", t=NT)
        gs_t2 = gsm[:, 112:128].rearrange("p (t n) -> p t n", t=NT)
        a_log = gsm[:, 128:136]
        dt_b = gsm[:, 136:144]
        sink = gsm[:, 144:160]
        ktl = gsm[:, 160:164]

        bank = ctx.enter_context(nc.psum_tensor("bank", [P, 8, CH], F32))

        def pair(n):
            return bank[:, 2 * n:2 * n + 2, :]

        def half(n):
            return bank[:, 6:8, :] if n % 2 == 0 else bank[:, 4:6, :]

        def flat(n):
            return half(n).rearrange("p b n -> p (b n)")

        loaded = sem("loaded")
        rows_zeroed = sem("rows_zeroed")
        x_landed = sem("x_landed")
        late = sem("late")
        ab_landed = sem("ab_landed")
        landed = [sem(f"landed{n}") for n in range(RAW)]
        ada_used = sem("ada_used")
        hi_ready = sem("hi_ready")
        lo_ready = sem("lo_ready")
        w_used = sem("w_used")
        taken = [sem(f"pair{n}_taken") for n in range(3)]
        made = sem("made")
        acc_zeroed = sem("acc_zeroed")
        ones_set = sem("ones_set")
        act_step = sem("act_step")
        dve_step = sem("dve_step")
        pool_step = sem("pool_step")
        cols_ready = sem("cols_ready")
        c_floor = sem("c_floor")
        c_exp = sem("c_exp")
        lb_sub = sem("lb_sub")
        lb_exp = sem("lb_exp")
        mod_ready = sem("mod_ready")
        norm_src = sem("norm_src")
        rms_raw = sem("rms_raw")
        xn_ready = sem("xn_ready")
        h32_ready = sem("h32_ready")
        op_hi = sem("op_hi")
        op_lo = sem("op_lo")
        stored = sem("stored")

        hg = {n: sem("hg_" + n) for n in (
            "zero", "q", "gf", "ff", "e", "f", "lf", "d", "exp", "qe", "ke", "pred", "kd", "kde", "qde", "kh", "qd", "kht", "s1",
            "ge", "gr", "gate", "sq", "ss", "rs", "on", "o", "hi", "lo")}
        gd = {n: sem("gd_" + n) for n in (
            "ab_hi", "ab_lo", "ab", "bf", "gf", "cf", "z", "ez", "lz", "eb", "ea", "la", "g", "eg", "conv", "ce", "silu", "sq", "lnp", "ln",
            "lab", "bb", "gc", "d", "ge", "ke", "ktl", "kb", "kk", "qk", "qde", "qd", "kg", "vb", "ct", "x", "xx", "p",
            "u", "wt", "s1", "vn", "gte", "gr", "gate", "osq", "ss", "rs", "on", "o", "hi", "lo")}
        gt_ready = sem("gt_ready")
        ff = {n: sem("ff_" + n) for n in ("act", "made", "hi", "lo", "zero")}
        att = {n: sem("att_" + n) for n in ("cv", "conv", "m", "hi", "lo", "kr", "qr", "kt", "qt", "s", "mx", "p", "pt",
                                            "es", "pv")}
        gate = {n: sem("gate_" + n) for n in ("rows", "z", "e", "r", "m", "made", "hi", "lo")}
        f2 = {n: sem("f2_" + n) for n in ("made", "cva", "cvg", "e", "z", "q", "h", "hi", "lo", "sum")}
        fin = {n: sem("fin_" + n) for n in ("rows", "out")}

        block = ctx.enter_context(nc.Block())

        class Steps:

            def __init__(self, eng, s):
                self.eng, self.s, self.n = eng, s, 0

            def link(self, ins):
                ins.then_inc(self.s, 1)
                self.n += 1
                self.eng.wait_ge(self.s, self.n)

            def mark(self, ins):
                ins.then_inc(self.s, 1)
                self.n += 1

            def wait(self):
                self.eng.wait_ge(self.s, self.n)

        def raw_landed(eng, s, j):
            eng.wait_ge(landed[j % RAW], 4 * (s + j - j % RAW) + 16)

        def split_hi(act, s, j, g, gj):
            raw_landed(act, s, j)
            if isinstance(g, int) and g + gj < RAW:
                pass
            else:
                act.wait_ge(w_used, g + gj - RAW + 1)
            nc.scalar.activation(w_hi[:, gj % RAW], raw[:, j % RAW], ACT.Copy).then_inc(hi_ready, 1)

        def split_lo(dve, g, gj, j):
            dve.wait_ge(hi_ready, g + gj + 1)
            nc.vector.tensor_tensor(w_lo[:, gj % RAW], raw[:, j % RAW], w_hi[:, gj % RAW].bitcast(F32),
                                    ALU.subtract).then_inc(lo_ready, 1)

        def piece(pe, g, gj, hi, lo, kt, where, first, last):
            s = gj % RAW
            pe.wait_ge(hi_ready, g + gj + 1)
            for k in range(PK):
                for t in range(NT):
                    tok = slice(t * P, (t + 1) * P)
                    nc.tensor.matmul(where[:, t], hi(kt + k, tok), w_hi[:, s, k], start=first and k == 0, stop=False)
                    nc.tensor.matmul(where[:, t], lo(kt + k, tok), w_hi[:, s, k], start=False, stop=False)
            pe.wait_ge(lo_ready, g + gj + 1)
            for k in range(PK):
                for t in range(NT):
                    mm = nc.tensor.matmul(where[:, t], hi(kt + k, slice(t * P, (t + 1) * P)), w_lo[:, s, k],
                                          start=False, stop=last and k == PK - 1)
            mm.then_inc(w_used, 1)

        def of(op):
            return (lambda kt, tok: op[0][:, kt, tok]), (lambda kt, tok: op[1][:, kt, tok])

        def of_b(base=0):
            return tuple((lambda kt, tok, x=x: op_b[(base + kt) // 8][x][:, (base + kt) % 8, tok]) for x in range(2))

        def chunk(pe, g, gj, op, kts, where, kt0=0):
            hi, lo = op
            n = kts // PK
            for k in range(n):
                piece(pe, g, gj + k, hi, lo, kt0 + PK * k, where, k == 0, k == n - 1)

        def load(sp, s, j, src):
            sp.dma_start(raw[:, j % RAW], src).then_inc(landed[j % RAW], 16)

        def w_piece(w, kt, c):
            if isinstance(kt, int):
                r = w[kt * P:(kt + PK) * P, :]
            else:
                r = w[bass.ds(kt * P, PK * P), :]
            return r.rearrange("(k p) n -> p k n", p=P)[:, :, bass.ds(c, CH)]

        w_ada, w_in, w_out, w_ff1, w_ff2 = (a[n][0] for n in ("w_ada", "w_in", "w_out", "w_ff1", "w_ff2"))
        w_in2, w_oa, w_oo, w_mx, w_up, w_dn = (a[n][0] for n in (
            "w_in_2", "w_out_a_2", "w_o_attn_2", "w_mix_out_2", "ffn_w_up_2", "ffn_w_down_2"))
        KP = KT // PK

        def bcast(src, n):
            return src.rearrange("(o n) -> o n", o=1).to_broadcast([P, n])

        x_in = a["x"][0].rearrange("(t p) d -> p t d", p=P)
        o_out = out[0].rearrange("(t p) d -> p t d", p=P)

        row_src = {
            "c": a["c"][0].rearrange("(r n) -> r n", n=P),
            "pre_mix": a["pre_mix_norm"][0].rearrange("(r n) -> r n", n=P),
            "pre_ffn": a["pre_ffn_norm"][0].rearrange("(r n) -> r n", n=P),
            "mix2": a["norm_mix_g_2"][0].rearrange("(r n) -> r n", n=P),
            "ffn2": a["norm_ffn_g_2"][0].rearrange("(r n) -> r n", n=P),
            "lb": a["hg_lb_logits"].rearrange("a h n -> (a h) n"),
            "conv_a": a["conv_a_w_2"][0].rearrange("k (r n) -> (k r) n", n=P),
            "gdn_conv": a["gdn_conv_w"][0].rearrange("k (r n) -> (k r) n", n=P),
            "ffn_conv0": a["ffn_conv_w_2"][0, 0].rearrange("(r n) -> r n", n=P),
            "ffn_conv1": a["ffn_conv_w_2"][0, 1].rearrange("(r n) -> r n", n=P),
            "ffn_conv2": a["ffn_conv_w_2"][0, 2].rearrange("(r n) -> r n", n=P),
            "ffn_bias": a["ffn_conv_b_2"][0].rearrange("(r n) -> r n", n=P),
            "b_ada": a["b_ada"][0].rearrange("(r n) -> r n", n=P),
        }
        N_LOADED = 16 * (1 + len(row_src) + 5)

        def ada_piece(q_col, kt, h):
            r = w_ada[bass.ds(kt * P, P), bass.ds(q_col + h * 2 * CH, 2 * CH)]
            return r.rearrange("p (k n) -> p k n", k=PK)

        @block.sync
        def _(sp):
            def load_w(name, sn, gn, j, src):
                sp.wait_ge(lo_ready, gn + j - RAW + 1)
                load(sp, sn, j, src)

            sp.dma_start(table[:], consts).then_inc(loaded, 16)
            sp.wait_ge(rows_zeroed, 1)
            for r, tile in enumerate(ROW_TILES):
                k = 0
                for name, n in tile:
                    sp.dma_start(rows[k:k + n, r], row_src[name]).then_inc(loaded, 16)
                    k += n
            sp.dma_start(head_norm[:, 0], bcast(a["hg_norm"][0], P)).then_inc(loaded, 16)
            sp.dma_start(head_norm[:, 1], bcast(a["gdn_norm"][0], P)).then_inc(loaded, 16)
            sp.dma_start(a_log, bcast(a["gdn_a_log"][0], HEADS)).then_inc(loaded, 16)
            sp.dma_start(dt_b, bcast(a["gdn_dt_bias"][0], HEADS)).then_inc(loaded, 16)
            sp.dma_start(sink, bcast(a["sink_logits_2"][0], AH)).then_inc(loaded, 16)
            sp.dma_start(X[:], x_in).then_inc(x_landed, 16)
            for j in range(4):
                load(sp, 0, j, ada_piece(0, 0, j))
            with sp.Fori(1, KT) as kt:
                for j in range(4):
                    sp.wait_ge(ada_used, 4 * kt + j - RAW + 1)
                    load(sp, 4 * kt, j, ada_piece(0, kt, j))
            sp.wait_ge(ada_used, 4 * KT)

            def mixed(name, col0, q_cols):
                a0 = 4 * KT + (0 if name == "hg" else 64)
                with sp.Fori(0, 2) as i:
                    s, g = STREAM[name] + 64 * i, GEMM[name] + 32 * i
                    for c in range(4):
                        for k in range(KP):
                            n = KP * c + k
                            sp.wait_ge(lo_ready, g + max(n - 1, 0))
                            load(sp, s, 2 * n, w_piece(w_in, PK * k, col0 + 4 * CH * i + CH * c))
                            sp.wait_ge(ada_used, a0 + 32 * i + n - 1)
                            load(sp, s, 2 * n + 1, ada_piece(q_cols(i), 4 * c + k // 2, k % 2))

            mixed("hg", 0, lambda i: 3 * D + i * D)
            mixed("gdn", HG_COLS, lambda i: 2 * D + i * (3 * D))
            sp.dma_start(ab_raw[:], w_in[:, HG_COLS + 4096:HG_COLS + 4112].rearrange("(k p) n -> p k n", p=P)) \
                .then_inc(ab_landed, 16)
            sp.wait_ge(lo_ready, GEMM["out"])
            sp.wait_ge(ada_used, 4 * KT + 128)
            with sp.Fori(0, 4) as c:
                for k in range(KP):
                    load_w("out", STREAM["out"] + KP * c, GEMM["out"] + KP * c, k, w_piece(w_out, PK * k, CH * c))
            sp.wait_ge(gd["lo"], GROUPS)
            sp.dma_start(gate_rows[:, 0], bcast(a["b_ada"][0, 2 * D:3 * D], D)).then_inc(late, 16)
            sp.dma_start(gate_rows[:, 1], bcast(a["post_mix_norm"][0], D)).then_inc(late, 16)
            sp.dma_start(gate_rows[:, 2], bcast(a["b_ada"][0, 5 * D:6 * D], D)).then_inc(late, 16)
            sp.dma_start(gate_rows[:, 3], bcast(a["post_ffn_norm"][0], D)).then_inc(late, 16)
            sp.dma_start(X[:], x_in).then_inc(x_landed, 16)
            s, g = STREAM["ffn"], GEMM["ffn"]
            for k in range(KP):
                load_w("ffn", s, g, k, w_piece(w_ff1, PK * k, 0))
            with sp.Fori(1, FF1 // CH) as i:
                si, gi = s - 8 + 16 * i, g - 8 + 16 * i
                for k in range(KP):
                    load_w("ffn", si, gi, k, w_piece(w_ff1, PK * k, CH * i))
                for c in range(4):
                    for k in range(2):
                        load_w("ffn", si, gi, KP + 2 * c + k, w_piece(w_ff2, 4 * i - 4 + PK * k, CH * c))
            for c in range(4):
                for k in range(2):
                    load_w("ffn", s + 248, g + 248, 2 * c + k, w_piece(w_ff2, FF1 // P - 4 + PK * k, CH * c))
            s, g = STREAM["in2"], GEMM["in2"]
            with sp.Fori(0, 9) as c:
                for k in range(KP):
                    load_w("in2", s + KP * c, g + KP * c, k, w_piece(w_in2, PK * k, CH * c))
            sp.wait_ge(att["lo"], 4)
            sp.dma_start(gbias[:, 0], bcast(a["b_gate_2"][0, 0:D], D)).then_inc(gate["rows"], 16)
            sp.dma_start(gbias[:, 1], bcast(a["b_gate_2"][0, D:2 * D], D)).then_inc(gate["rows"], 16)
            s, g = STREAM["gate"], GEMM["gate"]
            with sp.Fori(0, 4) as n:
                sn, gn = s + 24 * n, g + 24 * n
                for x in range(2):
                    for k in range(KP):
                        j = KP * x + k
                        sp.wait_ge(lo_ready, gn + j - RAW + 1 + (j == 2 * KP - 1))
                        load(sp, sn, j, w_piece(w_in2, PK * k, 9 * CH + D * x + CH * n))
                for x, w in enumerate((w_oa, w_oo)):
                    for k in range(4):
                        j = 2 * KP + 4 * x + k
                        if j > 2 * KP:
                            sp.wait_ge(lo_ready, gn + j - RAW + 1)
                        load(sp, sn, j, w_piece(w, PK * k, CH * n))
            s, g = STREAM["mix"], GEMM["mix"]
            with sp.Fori(0, 4) as c:
                for k in range(KP):
                    load_w("mix", s + KP * c, g + KP * c, k, w_piece(w_mx, PK * k, CH * c))
            s, g = STREAM["ffn2"], GEMM["ffn2"]
            for x in range(2):
                for k in range(KP):
                    load_w("ffn2", s, g, KP * x + k, w_piece(w_up, PK * k, FF2 * x))
            with sp.Fori(1, FF2 // CH) as i:
                si, gi = s - 8 + 24 * i, g - 8 + 24 * i
                for x in range(2):
                    for k in range(KP):
                        load_w("ffn2", si, gi, KP * x + k, w_piece(w_up, PK * k, FF2 * x + CH * i))
                for c in range(4):
                    for k in range(2):
                        load_w("ffn2", si, gi, 2 * KP + 2 * c + k, w_piece(w_dn, 4 * i - 4 + PK * k, CH * c))
            sp.dma_start(fin_norm[:], bcast(a["norm_final_g_2"], D)).then_inc(fin["rows"], 16)
            for c in range(4):
                for k in range(2):
                    load_w("ffn2", s + 256, g + 256, 2 * c + k, w_piece(w_dn, FF2 // P - 4 + PK * k, CH * c))
            for t in range(NT):
                sp.wait_ge(fin["out"], t + 1)
                sp.dma_start(o_out[:, t], XN[:, t]).then_inc(stored, 16)
            sp.wait_ge(stored, 16 * NT)

        @block.tensor
        def _(pe):
            reader = [None, None]

            def tile_free(n):
                if reader[n % 2] is not None:
                    pe.wait_ge(*reader[n % 2])

            def tile_done(mm, n, s, value):
                mm.then_inc(made, 1)
                reader[n % 2] = (s, value)

            def units(n, fn, s, value, count=UN):
                tile_free(n)
                for u in range(count):
                    mm = fn(u, flat(n)[:, u * P:(u + 1) * P])
                tile_done(mm, n, s, value)

            def turned(o, src):
                return nc.tensor.transpose(o, src, ident)

            def mul(o, l, r):
                return nc.tensor.matmul(o, l, r, start=True, stop=True)

            pe.wait_ge(loaded, N_LOADED)
            n = TILE[("rows", 0, "rows")]
            units(n, lambda u, o: turned(o, rows[:, u]), cols_ready, 1, 7)

            def column_sums(n, done):
                tile_free(n)
                for q in range(2):
                    for j in range(KT):
                        mm = mul(flat(n)[:, KT * q + j:KT * q + j + 1], acc[:, q, j * P:(j + 1) * P], ones[:, 0:1])
                tile_done(mm, n, mod_ready, done)

            pe.wait_ge(ones_set, 1)
            pe.wait_ge(ada_used, 4 * KT)
            column_sums(TILE[("mod", 0, "shsc")], 1)

            def turn_rows(name, k):
                pe.wait_ge(xn_ready, 2 * k + 2)
                for q in range(4):
                    n = TILE[(name, 0, f"t{q}")]
                    units(n, lambda u, o: turned(o, XN[:, u % NT, (4 * q + u // NT) * P:(4 * q + u // NT + 1) * P]),
                          h32_ready, 4 * k + q + 1)
                pe.wait_ge(op_hi, 4 * k + 4)
                pe.wait_ge(op_lo, 4 * k + 4)

            def plain(name, chunks, op):
                u = USES[name]
                with pe.Fori(0, chunks // 2) as i:
                    for x in range(2):
                        pe.wait_ge(taken[x], u[x] + i)
                        chunk(pe, GEMM[name] + 2 * KP * i, KP * x, op, KT, pair(x))
                if chunks % 2:
                    pe.wait_ge(taken[0], u[0] + chunks // 2)
                    chunk(pe, GEMM[name] + KP * (chunks - 1), 0, op, KT, pair(0))

            turn_rows("op0", 0)
            plain("hg", 8, of(op_a))

            pe.wait_ge(taken[0], USES["gdn"][0])
            pe.wait_ge(taken[1], USES["gdn"][1])
            Q, K, B, D0, D1, QE0, QE1, KE0, KE1, A, R = hg_t
            QE, KE = [QE0, QE1], [KE0, KE1]
            for g in range(GROUPS):
                def T(name):
                    return TILE[("hg", g, name)]

                def hcols(part, u):
                    h = g * GH + u // NT
                    return proj[:, u % NT, part * 1024 + h * P:part * 1024 + (h + 1) * P]

                units(T("q"), lambda u, o: turned(o, hcols(0, u)), hg["q"], g + 1)
                units(T("f"), lambda u, o: turned(o, hcols(1, u)), hg["ff"], g + 1)
                for lev in range(LEVELS):
                    pe.wait_ge(hg["qe"], LEVELS * g + lev + 1)
                    pe.wait_ge(hg["ke"], LEVELS * g + lev + 1)
                    units(T(f"lev{lev}"), lambda u, o: mul(o, KE[lev % 2][:, u], QE[lev % 2][:, u]),
                          hg["pred"], (LEVELS + 1) * g + lev + 1)
                units(T("diag"), lambda u, o: mul(o, K[:, u], Q[:, u]), hg["pred"], (LEVELS + 1) * (g + 1))
                pe.wait_ge(hg["kh"], g + 1)
                units(T("kh"), lambda j, o: turned(o, KE0[:, j]), hg["kht"], g + 1, GH)
                pe.wait_ge(hg["kht"], g + 1)
                units(T("s1"), lambda j, o: mul(o, KE0[:, GH + j], hcols(2, NT * j)), hg["s1"], g + 1, GH)
                pe.wait_ge(hg["pred"], (LEVELS + 1) * (g + 1))
                pe.wait_ge(hg["qd"], g + 1)
                pe.wait_ge(hg["s1"], g + 1)

                def hg_out(u, o):
                    j, t = u // NT, u % NT
                    mm = nc.tensor.matmul(o, A[:, u], hcols(2, u), start=True, stop=t == 0)
                    if t == 1:
                        mm = nc.tensor.matmul(o, QE0[:, j], QE0[:, GH + j], start=False, stop=True)
                    return mm

                units(T("o"), hg_out, hg["on"], g + 1)
                pe.wait_ge(hg["o"], g + 1)
                units(T("turn"), lambda u, o: turned(o, D1[:, u]), hg["lo"], g + 1)

            column_sums(TILE[("mod2", 0, "shsc")], 2)
            plain("gdn", 8, of(op_a))
            pe.wait_ge(gd["ab_lo"], 1)
            pe.wait_ge(taken[0], USES["ab"][0])
            for t in range(NT):
                tok = slice(t * P, (t + 1) * P)
                for kt in range(KT):
                    o = pair(0)[:, t, 0:16]
                    nc.tensor.matmul(o, op_a[0][:, kt, tok], ab_hi[:, kt], start=kt == 0, stop=False)
                    nc.tensor.matmul(o, op_a[1][:, kt, tok], ab_hi[:, kt], start=False, stop=False)
                    mm = nc.tensor.matmul(o, op_a[0][:, kt, tok], ab_lo[:, kt], start=False, stop=kt == KT - 1)
            mm.then_inc(gd["ab"], 1)

            QF, KF, VF, E, GM, MT, QK, CT, X_, XT, PP, VB, KG, QD, R2 = gd_t
            pe.wait_ge(gd["la"], 1)
            pe.wait_ge(taken[1], USES["out"][1])
            n = TILE[("gs", 0, "g")]
            tile_free(n)
            for t in range(NT):
                mm = mul(flat(n)[:, t * HEADS:(t + 1) * HEADS], upper, log_a[:, t])
            tile_done(mm, n, gd["g"], 1)
            for g in range(GROUPS):
                def T(name):
                    return TILE[("gdn", g, name)]

                def W(name, k=1, n=1):
                    pe.wait_ge(gd[name], g * n + k)

                def gcols(part, u):
                    h = g * GH + u // NT
                    return proj[:, u % NT, part * 1024 + h * P:part * 1024 + (h + 1) * P]

                for x, name in enumerate(("q", "k", "v")):
                    units(T(name), lambda u, o: turned(o, gcols(x, u)), gd["conv"], 3 * g + x + 1)
                for x, name in enumerate(("sq", "sk")):
                    W("sq", x + 1, 2)
                    n, src = T(name), [CT, X_][x]
                    tile_free(n)
                    for b in range(2):
                        mm = mul(half(n)[:, b], ones[:], src[:, 4 * b:4 * b + 4].rearrange("p u n -> p (u n)"))
                    tile_done(mm, n, gd["lnp"], 2 * g + x + 1)
                W("lab")
                units(T("grow"), lambda u, o: mul(o, XT[:, u], upper), gd["gc"], g + 1)
                W("bb")
                units(T("beta"), lambda u, o: mul(o, PP[:, u], ident), gd["kb"], g + 1)
                W("kb")
                units(T("kk"), lambda u, o: mul(o, KF[:, u], QD[:, u]), gd["kk"], g + 1)
                units(T("qk"), lambda u, o: mul(o, KF[:, u], QF[:, u]), gd["qk"], g + 1)
                units(T("kt"), lambda u, o: turned(o, KF[:, u]), gd["kg"], g + 1)
                units(T("vt"), lambda u, o: turned(o, VF[:, u]), gd["vb"], g + 1)
                W("ct", 1, LEVELS)
                units(T("p0"), lambda u, o: mul(o, CT[:, u], ident), gd["x"], LEVELS * g + 1)
                for lev in range(1, LEVELS):
                    ct = [CT, VF][lev % 2]
                    W("ct", lev + 1, LEVELS)
                    W("x", lev, LEVELS)
                    units(T(f"p{lev}"), lambda u, o: mul(o, ct[:, u], X_[:, u]), gd["p"], (LEVELS - 1) * g + lev)
                    W("p", lev, LEVELS - 1)
                    if lev < LEVELS - 1:
                        units(T(f"xp{lev}"), lambda u, o: mul(o, XT[:, u], PP[:, u]), gd["xx"], (LEVELS - 2) * g + lev)
                    units(T(f"px{lev}"), lambda u, o: mul(o, PP[:, u], XT[:, u]), gd["x"], LEVELS * g + lev + 1)
                W("x", LEVELS, LEVELS)
                W("vb")
                units(T("u"), lambda u, o: mul(o, XT[:, u], VB[:, u]), gd["u"], g + 1)
                W("kg")
                units(T("wt"), lambda j, o: mul(o, KG[:, j], XT[:, NT * j + 1]), gd["wt"], g + 1, GH)
                W("u")
                units(T("s1"), lambda j, o: mul(o, KG[:, GH + j], PP[:, NT * j]), gd["s1"], g + 1, GH)
                W("wt")
                W("s1")
                units(T("ws"), lambda j, o: mul(o, E[:, j], E[:, GH + j]), gd["vn"], g + 1, GH)
                W("vn")
                W("qd")
                W("qk")

                def gd_out(u, o):
                    j, t = u // NT, u % NT
                    mm = nc.tensor.matmul(o, QK[:, u], PP[:, u], start=True, stop=t == 0)
                    if t == 1:
                        mm = nc.tensor.matmul(o, QD[:, j], E[:, GH + j], start=False, stop=True)
                    return mm

                units(T("o"), gd_out, gd["on"], g + 1)
                W("o")
                units(T("turn"), lambda u, o: turned(o, X_[:, u]), gd["lo"], g + 1)

            pe.wait_ge(hg["lo"], GROUPS)
            pe.wait_ge(gd["lo"], GROUPS)
            plain("out", 4, of_b())
            for q in range(2):
                for h in range(2):
                    n = TILE[("gt", 0, "mf"[q] + str(h))]
                    tile_free(n)
                    for b in range(2):
                        mm = mul(half(n)[:, b], ones[:], acc[:, q, (2 * h + b) * CH:(2 * h + b + 1) * CH])
                    tile_done(mm, n, gt_ready, 2 * q + h + 1)
            turn_rows("op1", 1)

            u_ff = USES["ffn"]

            def turn_block(src, s):
                for kt in range(4):
                    for t in range(NT):
                        mm = turned(flat(0)[:, kt * SEQ + t * P:kt * SEQ + (t + 1) * P], src[:, t, kt * P:(kt + 1) * P])
                mm.then_inc(s, 1)

            def up(i, g):
                pe.wait_ge(taken[2], u_ff[2] + i)
                chunk(pe, g, 0, of(op_a), KT, pair(2))

            def down(i, g, gj, between=None):
                pe.wait_ge(ff["hi"], i + 1)
                pe.wait_ge(ff["lo"], i + 1)
                for c in range(4):
                    x = (c + 1) % 2
                    if c == 2 and between:
                        between()
                    pe.wait_ge(taken[x], u_ff[x] + 2 * i + c // 2)
                    chunk(pe, g, gj + 2 * c, of(hid), 4, pair(x))

            def turn_hidden(i):
                pe.wait_ge(ff["act"], i + 1)
                turn_block(relu, ff["made"])

            g0 = GEMM["ffn"]
            up(0, g0)
            turn_hidden(0)
            with pe.Fori(1, FF1 // CH) as i:
                up(i, g0 - 8 + 16 * i)
                down(i - 1, g0 - 8 + 16 * i, KP, lambda: turn_hidden(i))
            down(FF1 // CH - 1, g0 + 248, 0)

            turn_rows("op2", 2)
            plain("in2", 9, of(op_a))
            for g in range(2):
                pe.wait_ge(att["cv"], g + 1)
                pe.wait_ge(taken[0], USES["gate"][0])
                for name, c0, s in (("cv", (2 + g) * CH, "conv"), ("b", g * CH, "m")):
                    units(TILE[("att", 0, f"{name}{g}")],
                          lambda u, o: turned(o, proj2[:, u % NT, c0 + (u // NT) * P:c0 + (u // NT + 1) * P]),
                          att[s], g + 1)
            S, KR, PT, QTs, KTs = at_t[0:2], at_t[2], at_t[2:4], at_t[4:6], at_t[6]
            pe.wait_ge(att["kr"], 1)
            units(TILE[("att", 0, "kt")], lambda u, o: turned(o, KR[:, (u % NT) * 4 + u // NT]), att["kt"], 1)
            pe.wait_ge(att["qr"], 1)
            for b in range(2):
                units(TILE[("att", 0, f"qt{b}")], lambda u, o: turned(o, S[u % NT][:, 4 * b + u // NT]), att["qt"], b + 1)
            pe.wait_ge(att["kt"], 1)
            pe.wait_ge(att["qt"], 2)

            def scores(b):
                kv, t = b // 2, b % 2
                n = TILE[("att", 0, f"sc{b}")]
                tile_free(n)
                for par in range(2):
                    part = slice(AD * par, AD * par + AD)
                    for x in range(2):
                        pr = 2 * kv + x
                        mm = mul(half(n)[:, par, x * SEQ:(x + 1) * SEQ], QTs[pr // 4][part, NT * (pr % 4) + t],
                                 KTs[part, NT * kv:NT * kv + NT].rearrange("p t n -> p (t n)"))
                tile_done(mm, n, att["s"], b + 1)

            def probs_values(b):
                kv = b // 2
                pe.wait_ge(att["p"], b + 1)
                units(TILE[("att", 0, f"pt{b}")], lambda u, o: turned(o, S[b % 2][:, u]), att["pt"], b + 1)
                pe.wait_ge(att["pt"], b + 1)
                n = TILE[("att", 0, f"pv{b}")]
                tile_free(n)
                for u in range(4):
                    for kb in range(2):
                        v = proj2[:, kb, 8 * CH + 256 + kv * AD:8 * CH + 256 + (kv + 1) * AD]
                        mm = nc.tensor.matmul(flat(n)[:, u * AD:(u + 1) * AD], PT[b % 2][:, 2 * u + kb], v,
                                              start=kb == 0, stop=kb == 1)
                tile_done(mm, n, att["pv"], b + 1)

            scores(0)
            for b in range(8):
                if b < 7:
                    scores(b + 1)
                probs_values(b)
            pe.wait_ge(att["pv"], 8)
            for x in range(2):
                units(TILE[("att", 0, f"at{x}")],
                      lambda u, o: turned(o, proj2[:, u % NT, 6 * CH + (4 * x + u // NT) * P:6 * CH + (4 * x + u // NT + 1) * P]),
                      att["lo"], 3 + x)
            pe.wait_ge(att["lo"], 4)

            u_ga = USES["gate"]

            def gate_chunk(n, turn_before):
                g = GEMM["gate"] + 24 * n
                pe.wait_ge(taken[0], u_ga[0] + 2 * n)
                chunk(pe, g, 0, of(op_a), KT, pair(0))
                if turn_before:
                    turn_mixed(n - 1)
                pe.wait_ge(taken[1], u_ga[1] + 2 * n)
                chunk(pe, g, 8, of(op_a), KT, pair(1))
                pe.wait_ge(taken[0], u_ga[0] + 2 * n + 1)
                chunk(pe, g, 16, of_b(), 8, pair(0))
                pe.wait_ge(taken[1], u_ga[1] + 2 * n + 1)
                chunk(pe, g, 20, of_b(8), 8, pair(1))

            def turn_mixed(n):
                pe.wait_ge(gate["m"], n + 1)
                pe.wait_ge(gate["lo"], n)
                turn_block(ma[:, 0], gate["made"])

            gate_chunk(0, False)
            with pe.Fori(1, 4) as n:
                gate_chunk(n, True)
            turn_mixed(3)
            pe.wait_ge(gate["hi"], 4)
            pe.wait_ge(gate["lo"], 4)
            plain("mix", 4, of(op_c))
            turn_rows("op3", 3)

            u_f2 = USES["ffn2"]

            def up2(i, g):
                pe.wait_ge(taken[2], u_f2[2] + i)
                chunk(pe, g, 0, of(op_a), KT, pair(2))
                pe.wait_ge(taken[0], before_gate(i))
                chunk(pe, g, 8, of(op_a), KT, pair(0))

            def before_gate(i):
                return u_f2[0] if isinstance(i, int) and i == 0 else u_f2[0] + 3 * i - 2

            def down2(i, g, gj, last=False, between=None):
                pe.wait_ge(f2["hi"], i + 1)
                pe.wait_ge(f2["lo"], i + 1)
                for c in range(4):
                    x = (c + 1) % 2
                    if c == 2 and between:
                        between()
                    if x == 1:
                        pe.wait_ge(taken[1], u_f2[1] + 2 * i + c // 2)
                    else:
                        pe.wait_ge(taken[0], u_f2[0] + 3 * i + (1 if last else 2) + c // 2)
                    chunk(pe, g, gj + 2 * c, of(hid2), 4, pair(x))

            def turn_up(i, k):
                if k == 1:
                    pe.wait_ge(taken[0], before_gate(i) + 1)
                    pe.wait_ge(f2["cva"], i + 1)
                    turn_block(up_g, f2["made"])
                else:
                    pe.wait_ge(taken[2], u_f2[2] + i + 1)
                    if not (isinstance(i, int) and i == 0):
                        pe.wait_ge(f2["cvg"], i)
                    turn_block(up_a, f2["made"])

            g0 = GEMM["ffn2"]
            up2(0, g0)
            turn_up(0, 0)
            turn_up(0, 1)
            with pe.Fori(1, FF2 // CH) as i:
                up2(i, g0 - 8 + 24 * i)
                turn_up(i, 0)
                down2(i - 1, g0 - 8 + 24 * i, 16, between=lambda: turn_up(i, 1))
            down2(FF2 // CH - 1, g0 + 256, 0, last=True)

        @block.scalar
        def _(act):
            st = Steps(act, act_step)

            def take(n):
                act.wait_ge(made, n + 1)

            def f(dst, src, func, s=None, **kw):
                ins = nc.scalar.activation(dst, src, func, **kw)
                return ins if s is None else ins.then_inc(s, 1)

            def tile(t, lo=0, hi=UN):
                return t[:, lo:hi].rearrange("p u n -> p (u n)")

            take(TILE[("rows", 0, "rows")])
            f(cols[:].rearrange("p a n -> p (a n)"), flat(0)[:, 0:7 * P], ACT.Copy, cols_ready)
            act.wait_ge(cols_ready, 1)
            act.wait_ge(c_floor, 1)
            f(tmp16, tmp16, ACT.Exp, c_exp, scale=-1.0)
            act.wait_ge(lb_sub, 1)
            f(lb, lb, ACT.Exp, lb_exp)
            f(one_lb, one_lb, ACT.Exp, lb_exp)

            def rms(src, *waits):
                for w in waits:
                    act.wait_ge(*w)
                for t in range(NT):
                    st.link(f(junk[:], src[:, t], ACT.Square, accum_out=sq_sum[:, t:t + 1]))
                st.link(f(r_a, sq_sum, ACT.Ln, scale=1.0 / D, bias=eps))
                f(rstd, r_a, ACT.Exp, rms_raw, scale=-0.5)

            def round_rows(k):
                for q in range(4):
                    act.wait_ge(h32_ready, 4 * k + q + 1)
                    f(op_a[0][:, 4 * q:4 * q + 4], H32[:, q % 2], ACT.Copy, op_hi)

            act.wait_ge(ones_set, 1)
            rms(X, (x_landed, 16))
            round_rows(0)

            def product(name, chunks, dst, per=1):
                def evacuate(n, x, g):
                    act.wait_ge(w_used, g)
                    f(dst(n), pair(x), ACT.Copy, taken[x])

                def one(n, x, prev):
                    g, s = GEMM[name] + KP * n, STREAM[name] + per * KP * n
                    for k in range(KP):
                        split_hi(act, s, per * k, g, k)
                        if k == 2 and prev is not None:
                            evacuate(prev, 1 - x, g)

                one(0, 0, None)
                one(1, 1, 0)
                if chunks > 4:
                    with act.Fori(1, chunks // 2) as i:
                        one(2 * i, 0, 2 * i - 1)
                        one(2 * i + 1, 1, 2 * i)
                else:
                    one(2, 0, 1)
                    one(3, 1, 2)
                if chunks % 2:
                    one(chunks - 1, 0, chunks - 2)
                evacuate(chunks - 1, (chunks - 1) % 2, GEMM[name] + KP * chunks)

            product("hg", 8, lambda n: proj[:, :, bass.ds(CH * n, CH)], per=2)

            def gate_exp(dst, g, s):
                act.wait_ge(s["gf"], g + 1)
                f(dst[:], dst[:], ACT.Exp, s["ge" if s is hg else "gte"], scale=-1.0)

            def finish_heads(s, g, T, squares, sq, dst):
                take(T("o"))
                f(tile(squares), flat(T("o")), ACT.Square, s[sq])
                act.wait_ge(s["ss"], g + 1)
                st.link(f(hrstd, hsum, ACT.Ln, scale=1.0 / P, bias=eps))
                f(hrstd, hrstd, ACT.Exp, s["rs"], scale=-0.5)
                take(T("turn"))
                f(dst[:, GH * g:GH * g + GH].rearrange("p j n -> p (j n)"), flat(T("turn")), ACT.Copy, s["hi"])

            Q, K, B, D0, D1, QE0, QE1, KE0, KE1, A, R = hg_t
            DD = [D0, D1]
            for g in range(GROUPS):
                def T(name):
                    return TILE[("hg", g, name)]

                if g:
                    act.wait_ge(hg["lo"], g)
                take(T("q"))
                f(tile(Q), flat(T("q")), ACT.Copy, hg["q"])
                act.wait_ge(hg["ff"], g + 1)
                f(D0[:], D0[:], ACT.Exp, hg["e"], scale=-1.0)
                gate_exp(R, g, hg)
                act.wait_ge(hg["f"], g + 1)
                f(D0[:], D1[:], ACT.Ln, hg["lf"])
                for lev in range(LEVELS):
                    act.wait_ge(hg["d"], LEVELS * g + lev + 1)
                    f(DD[lev % 2][:], DD[lev % 2][:], ACT.Exp, hg["exp"])
                act.wait_ge(hg["kd"], g + 1)
                f(D0[:, 0:GH], D0[:, 0:GH], ACT.Exp, hg["kde"])
                f(D0[:, GH:UN], B[:].rearrange("p (j t) n -> p j t n", t=NT)[:, :, 1], ACT.Exp, hg["qde"])
                take(T("kh"))
                f(tile(KE0, GH), flat(T("kh"))[:, 0:GH * P], ACT.Copy, hg["kht"])
                act.wait_ge(hg["qd"], g + 1)
                take(T("s1"))
                f(tile(QE0, GH), flat(T("s1"))[:, 0:GH * P], ACT.Copy, hg["s1"])
                finish_heads(hg, g, T, D0, "sq", op_b[0][0])

            product("gdn", 8, lambda n: proj[:, :, bass.ds(CH * n, CH)], per=2)

            QF, KF, VF, E, GM, MT, QK, CT, X_, XT, PP, VB, KG, QD, R2 = gd_t
            act.wait_ge(ab_landed, 16)
            f(ab_hi[:], ab_raw[:], ACT.Copy, gd["ab_hi"])
            act.wait_ge(gd["ab"], 1)
            f(ab, pair(0)[:, :, 0:16], ACT.Copy, taken[0])
            act.wait_ge(taken[0], USES["out"][0])
            act.wait_ge(gd["bf"], 1)
            f(beta, beta, ACT.Exp, gd["eb"], scale=-1.0)
            f(a_log, a_log, ACT.Exp, gd["ea"])
            act.wait_ge(gd["z"], 1)
            f(gs_t2, gs_t2, ACT.Exp, gd["ez"], scale=-1.0)
            act.wait_ge(gd["ez"], 1)
            f(gs_t2, gs_t2, ACT.Ln, gd["lz"], bias=ones[:, 0:1])
            act.wait_ge(gd["g"], 1)
            f(bg, g_cum, ACT.Exp, gd["eg"])
            for g in range(GROUPS):
                def T(name):
                    return TILE[("gdn", g, name)]

                def W(name, k=1, n=1):
                    act.wait_ge(gd[name], g * n + k)

                for x, (c, e) in enumerate(((QF, CT), (KF, X_), (VF, XT))):
                    W("cf", x + 1, 3)
                    f(e[:], e[:], ACT.Exp, gd["ce"], scale=-1.0)
                for x, (c, e) in enumerate(((QF, CT), (KF, X_))):
                    W("silu", x + 1, 3)
                    f(e[:], c[:], ACT.Square, gd["sq"])
                for x, (name, e) in enumerate((("sq", CT), ("sk", X_))):
                    take(T(name))
                    f(tile(e), flat(T(name)), ACT.Ln, gd["lnp"], bias=eps)
                    W("lnp", x + 1, 2)
                    f(tile(e), tile(e), ACT.Exp, gd["ln"], scale=-0.5)
                gate_exp(R2, g, gd)
                take(T("grow"))
                f(tile(VB), flat(T("grow")), ACT.Copy, gd["gc"])
                W("d")
                f(GM[:], GM[:], ACT.Exp, gd["ge"])
                W("ke")
                f(ktl, ktl, ACT.Exp, gd["ktl"])
                W("kk")
                f(QD[:, GH:UN], VB[:].rearrange("p (j t) n -> p j t n", t=NT)[:, :, 1], ACT.Exp, gd["qde"])
                for lev in range(1, LEVELS):
                    take(T(f"p{lev}"))
                    f(tile(PP), flat(T(f"p{lev}")), ACT.Copy, gd["p"])
                take(T("u"))
                f(tile(PP), flat(T("u")), ACT.Copy, gd["u"])
                take(T("wt"))
                f(tile(E, 0, GH), flat(T("wt"))[:, 0:GH * P], ACT.Copy, gd["wt"])
                take(T("s1"))
                f(tile(E, GH), flat(T("s1"))[:, 0:GH * P], ACT.Copy, gd["s1"])
                finish_heads(gd, g, T, XT, "osq", op_b[1][0])

            product("out", 4, lambda n: Y[:, :, bass.ds(CH * n, CH)])
            rms(Y, (taken[0], USES["ffn"][0]), (taken[1], USES["ffn"][1]))
            rms(X, (norm_src, 1))
            round_rows(1)

            def hi_pieces(s, g, n, hooks):
                for k in range(n):
                    split_hi(act, s, k, g, k)
                    if k in hooks:
                        hooks[k]()

            def relu_up(i, g):
                act.wait_ge(w_used, g + KP)
                act.wait_ge(ff["made"], i)
                f(relu[:], pair(2), ACT.Relu, taken[2])
                act.wait_ge(taken[2], USES["ffn"][2] + i + 1)
                f(relu[:], relu[:], ACT.Square, ff["act"])

            def round_hidden(i, g):
                act.wait_ge(ff["made"], i + 1)
                act.wait_ge(w_used, g)
                f(hid[0][:].rearrange("p k n -> p (k n)"), flat(0), ACT.Copy, ff["hi"])

            s0, g0 = STREAM["ffn"], GEMM["ffn"]
            hi_pieces(s0, g0, KP, {})

            def ffn_turn(i, first=False):
                g = g0 - 8 + 16 * i
                hooks = {5: lambda: round_hidden(i - 1, g), 11: lambda: relu_up(i, g)}
                if first:
                    hooks[2] = lambda: relu_up(0, g0)
                hi_pieces(s0 - 8 + 16 * i, g, 16, hooks)

            ffn_turn(1, True)
            with act.Fori(2, FF1 // CH) as i:
                ffn_turn(i)
            hi_pieces(s0 + 248, g0 + 248, 8, {2: lambda: round_hidden(FF1 // CH - 1, g0 + 248)})
            u = USES["in2"]
            rms(Y, (taken[0], u[0]), (taken[1], u[1]))
            rms(X, (norm_src, 2))
            round_rows(2)

            product("in2", 9, lambda n: proj2[:, :, bass.ds(CH * n, CH)])
            S, PT, QTs, KTs = at_t[0:2], at_t[2:4], at_t[4:6], at_t[6]
            for g in range(2):
                act.wait_ge(att["m"], g + 1)
                f(op_b[0][0][:, 4 * g:4 * g + 4].rearrange("p k n -> p (k n)"), tile(at_t[1]), ACT.Copy, att["hi"])
            take(TILE[("att", 0, "kt")])
            f(tile(KTs), flat(TILE[("att", 0, "kt")]), ACT.Copy, att["kt"])
            for b in range(2):
                n = TILE[("att", 0, f"qt{b}")]
                take(n)
                f(tile(QTs[b]), flat(n), ACT.Copy, att["qt"])

            def probs(b):
                act.wait_ge(att["mx"], b + 1)
                for x in range(4):
                    sc = S[b % 2][:, 2 * x:2 * x + 2].rearrange("p u n -> p (u n)")
                    ins = f(sc, sc, ACT.Exp, bias=k_nm[:, 4 * (b % 2) + x:4 * (b % 2) + x + 1],
                            accum_out=k_sum[:, 4 * (b % 2) + x:4 * (b % 2) + x + 1])
                ins.then_inc(att["p"], 1)
                e = k_es[:, 4 * (b % 2):4 * (b % 2) + 4]
                f(e, e, ACT.Exp, att["es"])

            probs(0)
            for b in range(8):
                if b < 7:
                    probs(b + 1)
                n = TILE[("att", 0, f"pt{b}")]
                take(n)
                f(tile(PT[b % 2]), flat(n), ACT.Copy, att["pt"])
            for x in range(2):
                n = TILE[("att", 0, f"at{x}")]
                take(n)
                f(op_b[1][0][:, 4 * x:4 * x + 4].rearrange("p k n -> p (k n)"), flat(n), ACT.Copy, att["hi"])

            def round_mixed(n):
                act.wait_ge(gate["made"], n + 1)
                f(op_c[0][:, bass.ds(4 * n, 4)].rearrange("p k n -> p (k n)"), flat(0), ACT.Copy, gate["hi"])

            def gate_exp2(n, x, z):
                act.wait_ge(gate["z"], 2 * n + x + 1)
                f(z[:], z[:], ACT.Exp, gate["e"], scale=-1.0)

            s0, g0 = STREAM["gate"], GEMM["gate"]

            def gate_turn(n, first=False):
                hooks = {13: lambda: gate_exp2(n, 0, za), 21: lambda: gate_exp2(n, 1, zb)}
                if not first:
                    hooks[11] = lambda: round_mixed(n - 1)
                hi_pieces(s0 + 24 * n, g0 + 24 * n, 24, hooks)

            gate_turn(0, True)
            with act.Fori(1, 4) as n:
                gate_turn(n)
            round_mixed(3)
            with act.Fori(0, 4) as c:
                hi_pieces(STREAM["mix"] + KP * c, GEMM["mix"] + KP * c, KP, {})
            u = USES["ffn2"]
            rms(X, (taken[0], u[0]), (taken[1], u[1]))
            round_rows(3)

            s0, g0 = STREAM["ffn2"], GEMM["ffn2"]

            def take_up(i, k, g):
                act.wait_ge(w_used, g)
                if not (isinstance(i, int) and i == 0):
                    act.wait_ge(f2["made"], 2 * i - 1 + k)
                f((up_a, up_g)[k][:], pair((2, 0)[k]), ACT.Copy, taken[(2, 0)[k]])

            def silu_exp(i):
                act.wait_ge(f2["z"], i + 1)
                f(sga[:], sga[:], ACT.Exp, f2["e"], scale=-1.0)

            def round_hidden2(i, g):
                act.wait_ge(f2["h"], i + 1)
                act.wait_ge(w_used, g)
                f(hid2[0][:], sga[:], ACT.Copy, f2["hi"])

            hi_pieces(s0, g0, 16, {11: lambda: take_up(0, 0, g0 + 8)})

            def ffn2_turn(i, first=False):
                g = g0 - 8 + 24 * i
                hooks = {3: lambda: silu_exp(i - 1), 7: lambda: round_hidden2(i - 1, g),
                         11: lambda: take_up(i, 0, g + 8), 19: lambda: take_up(i, 1, g + 16)}
                if first:
                    hooks[2] = lambda: take_up(0, 1, g0 + 16)
                hi_pieces(s0 - 8 + 24 * i, g, 24, hooks)

            ffn2_turn(1, True)
            with act.Fori(2, FF2 // CH) as i:
                ffn2_turn(i)
            n = FF2 // CH - 1
            hi_pieces(s0 + 256, g0 + 256, 8, {1: lambda: silu_exp(n), 3: lambda: round_hidden2(n, g0 + 256)})
            rms(X, (taken[0], _u[0]), (taken[1], _u[1]))

        @block.vector
        def _(dve):
            v = nc.vector
            st = Steps(dve, dve_step)

            def take(n):
                dve.wait_ge(made, n + 1)

            def tile(t, lo=0, hi=UN):
                return t[:, lo:hi].rearrange("p u n -> p (u n)")

            def over(scalars, n=UN):
                return scalars.unsqueeze(2).to_broadcast([P, n, P])

            def tt(out_, x, y, op, s=None):
                ins = v.tensor_tensor(out_, x, y, op)
                return ins if s is None else ins.then_inc(s, 1)

            def sigmoid_tail(t):
                st.link(v.tensor_scalar(t, t, 1.0, None, ALU.add))
                st.link(v.reciprocal(t, t))

            v.memset(eps, EPS)
            v.memset(ones[:], 1.0).then_inc(ones_set, 1)
            dve.wait_ge(cols_ready, 1)
            v.tensor_scalar(tmp16, col("c"), LOWEST, None, ALU.max).then_inc(c_floor, 1)
            lg = col("lb")
            st.link(tt(one_lb, lg[:, 0:HEADS], lg[:, HEADS:], ALU.max))
            st.link(tt(lb, lg[:, 0:HEADS], one_lb, ALU.subtract))
            tt(one_lb, lg[:, HEADS:], one_lb, ALU.subtract, lb_sub)
            dve.wait_ge(c_exp, 1)
            sigmoid_tail(tmp16)
            st.link(tt(c_act, col("c"), tmp16, ALU.mult))
            dve.wait_ge(lb_exp, 2)
            st.link(tt(one_lb, lb, one_lb, ALU.add))
            st.link(v.reciprocal(one_lb, one_lb))
            st.link(tt(lb, lb, one_lb, ALU.mult))
            st.link(v.tensor_scalar(one_lb, lb, -1.0, 1.0, ALU.mult, ALU.add))

            def add_ada(slot, kt, dst):
                v.scalar_tensor_tensor(out=dst, in0=raw[:, slot].rearrange("p k n -> p (k n)"), scalar=kt, in1=dst,
                                       op0=ALU.mult, op1=ALU.add).then_inc(ada_used, 1)

            dve.wait_ge(acc_zeroed, 1)
            with dve.Fori(0, KT) as kt:
                dve.wait_ge(ada_used, 4 * kt)
                for j in range(4):
                    raw_landed(dve, 4 * kt, j)
                    add_ada(j, c_act[:, bass.ds(kt, 1)], acc[:, j // 2, (j % 2) * 1024:(j % 2 + 1) * 1024])

            bias = col("b_ada")

            def modulation(n, shift, scale, b0, gain):
                take(n)
                st.link(tt(shift, flat(n)[:, 0:KT], bias[:, b0:b0 + KT], ALU.add))
                tt(scale, flat(n)[:, KT:2 * KT], bias[:, b0 + KT:b0 + 2 * KT], ALU.add, mod_ready)
                dve.wait_ge(mod_ready, 1 if b0 == 0 else 2)
                st.link(v.scalar_tensor_tensor(out=scale, in0=scale, scalar=1.0, in1=gain, op0=ALU.add, op1=ALU.mult))

            modulation(TILE[("mod", 0, "shsc")], shift_m, scale_m, 0, col("pre_mix"))

            def newton(k):
                dve.wait_ge(rms_raw, k + 1)
                st.link(v.tensor_scalar(r_ms, sq_sum, 1.0 / D, EPS, ALU.mult, ALU.add))
                st.link(tt(r_b, rstd, rstd, ALU.mult))
                st.link(tt(r_b, r_b, r_ms, ALU.mult))
                st.link(v.tensor_scalar(r_b, r_b, -0.5, 1.5, ALU.mult, ALU.add))
                st.link(tt(r_n, rstd, r_b, ALU.mult))

            def operand(name, k, r, scale, shift):
                newton(r)
                for t in range(NT):
                    v.tensor_scalar(XN[:, t], X[:, t], r_n[:, t:t + 1], None, ALU.mult).then_inc(xn_ready, 1)

                def low(q):
                    dve.wait_ge(op_hi, 4 * k + q + 1)
                    tt(op_a[1][:, 4 * q:4 * q + 4], H32[:, q % 2], op_a[0][:, 4 * q:4 * q + 4].bitcast(F32), ALU.subtract, op_lo)

                for q in range(4):
                    n = TILE[(name, 0, f"t{q}")]
                    take(n)
                    if q >= 2:
                        dve.wait_ge(op_lo, 4 * k + q - 1)
                    for kt in range(4):
                        x = 4 * q + kt
                        src = flat(n)[:, kt * SEQ:(kt + 1) * SEQ]
                        if shift is None:
                            ins = v.tensor_scalar(H32[:, q % 2, kt], src, scale[:, x:x + 1], None, ALU.mult)
                        else:
                            ins = v.tensor_scalar(H32[:, q % 2, kt], src, scale[:, x:x + 1], shift[:, x:x + 1],
                                                  ALU.mult, ALU.add)
                    ins.then_inc(h32_ready, 1)
                    if q:
                        low(q - 1)
                low(3)

            operand("op0", 0, 0, scale_m, shift_m)

            def mixed(name):
                a0 = 4 * KT + (0 if name == "hg" else 64)
                dve.wait_ge(acc_zeroed, 2 if name == "hg" else 3)
                with dve.Fori(0, 2) as i:
                    s, g = STREAM[name] + 64 * i, GEMM[name] + 32 * i
                    for n in range(4 * KP):
                        split_lo(dve, g, n, 2 * n)
                        raw_landed(dve, s, 2 * n + 1)
                        dve.wait_ge(ada_used, a0 + 32 * i + n - 1)
                        kt = 4 * (n // KP) + (n % KP) // 2
                        add_ada((2 * n + 1) % RAW, c_act[:, kt:kt + 1],
                                acc[:, bass.ds(i, 1), (n % 2) * 1024:(n % 2 + 1) * 1024].rearrange("p o n -> p (o n)"))

            mixed("hg")

            def gate_finish(s, g, R_):
                dve.wait_ge(s["ge" if s is hg else "gte"], g + 1)
                st.link(v.tensor_scalar(tile(R_), tile(R_), 1.0, None, ALU.add))
                v.reciprocal(tile(R_), tile(R_)).then_inc(s["gr"], 1)

            def finish_heads(s, g, T, squares, sq, res, R_, dst, k0):
                dve.wait_ge(s[sq], g + 1)
                v.tensor_reduce(hsum, squares[:], AX.X, ALU.add).then_inc(s["ss"], 1)
                dve.wait_ge(s["rs"], g + 1)
                tt(res[:], flat(T("o")).rearrange("p (u n) -> p u n", n=P), over(hrstd), ALU.mult, s["on"])
                dve.wait_ge(s["on"], g + 1)
                dve.wait_ge(s["gate"], g + 1)
                tt(res[:], res[:], R_[:], ALU.mult, s["o"])
                dve.wait_ge(s["hi"], g + 1)
                tt(dst[1][:, GH * g:GH * g + GH].rearrange("p j n -> p (j n)"), flat(T("turn")),
                   dst[0][:, GH * g:GH * g + GH].rearrange("p j n -> p (j n)").bitcast(F32), ALU.subtract, s["lo"])

            Q, K, B, D0, D1, QE0, QE1, KE0, KE1, A, R = hg_t
            DD, QE = [D0, D1], [QE0, QE1]

            def blocks(t, lev):
                return tile(t).rearrange("p (b n) -> p b n", n=2 << lev)

            dve.wait_ge(hg["zero"], 1)
            for g in range(GROUPS):
                def T(name):
                    return TILE[("hg", g, name)]

                take(T("f"))
                v.tensor_scalar(tile(D0), flat(T("f")), LOWEST, None, ALU.max).then_inc(hg["ff"], 1)
                dve.wait_ge(hg["e"], g + 1)
                sigmoid_tail(tile(D0))
                for j in range(GH):
                    h = g * GH + j
                    ins = v.tensor_scalar(D1[:, NT * j:NT * j + NT], D0[:, NT * j:NT * j + NT], one_lb[:, h:h + 1],
                                          lb[:, h:h + 1], ALU.mult, ALU.add)
                ins.then_inc(hg["f"], 1)
                dve.wait_ge(hg["f"], g + 1)
                st.link(v.tensor_scalar(K[:], D1[:], -1.0, 1.0, ALU.mult, ALU.add))
                dve.wait_ge(hg["lf"], g + 1)
                for u in range(UN):
                    ins = v.tensor_tensor_scan(B[:, u], ones[:], D0[:, u], 0.0, ALU.mult, ALU.add)
                st.link(ins)
                gate_finish(hg, g, R)

                def distance(lev):
                    h = 1 << lev
                    if lev >= 2:
                        dve.wait_ge(hg["ke"], LEVELS * g + lev - 1)
                        dve.wait_ge(hg["qe"], LEVELS * g + lev - 1)
                    b, d = blocks(B, lev), blocks(DD[lev % 2], lev)
                    ref = b[:, :, h - 1:h].to_broadcast([P, UN * P // (2 * h), h])
                    tt(d[:, :, h:], b[:, :, h:], ref, ALU.subtract)
                    tt(d[:, :, :h], ref, b[:, :, :h], ALU.subtract, hg["d"])

                def query_side(lev):
                    h = 1 << lev
                    dve.wait_ge(hg["exp"], LEVELS * g + lev + 1)
                    if lev >= 2:
                        take(T(f"lev{lev - 2}"))
                    tt(blocks(QE[lev % 2], lev)[:, :, h:], blocks(Q, lev)[:, :, h:], blocks(DD[lev % 2], lev)[:, :, h:],
                       ALU.mult, hg["qe"])

                def place(k, name, mask):
                    take(T(name))
                    dve.wait_ge(hg["pred"], (LEVELS + 1) * g + k)
                    v.copy_predicated(A[:], mask.bitcast(U32).unsqueeze(1).to_broadcast([P, UN, P]),
                                      flat(T(name)).rearrange("p (u n) -> p u n", n=P)).then_inc(hg["pred"], 1)

                distance(0)
                for lev in range(LEVELS):
                    if lev + 1 < LEVELS:
                        distance(lev + 1)
                    query_side(lev)
                    if lev:
                        place(lev - 1, f"lev{lev - 1}", level(lev - 1))
                place(LEVELS - 1, f"lev{LEVELS - 1}", level(LEVELS - 1))
                place(LEVELS, "diag", ident)
                dve.wait_ge(hg["ke"], LEVELS * g + LEVELS)
                b = B[:].rearrange("p (j t) n -> p j t n", t=NT)
                tt(D0[:, 0:GH], b[:, :, 0, P - 1:P].to_broadcast([P, GH, P]), b[:, :, 0], ALU.subtract, hg["kd"])
                dve.wait_ge(hg["kde"], g + 1)
                tt(KE0[:, 0:GH], K[:].rearrange("p (j t) n -> p j t n", t=NT)[:, :, 0], D0[:, 0:GH], ALU.mult, hg["kh"])
                dve.wait_ge(hg["qde"], g + 1)
                tt(QE0[:, 0:GH], Q[:].rearrange("p (j t) n -> p j t n", t=NT)[:, :, 1], D0[:, GH:UN], ALU.mult, hg["qd"])
                finish_heads(hg, g, T, D0, "sq", D1, R, op_b[0], 0)

            modulation(TILE[("mod2", 0, "shsc")], shift_f, scale_f, 3 * KT, col("pre_ffn"))
            mixed("gdn")

            QF, KF, VF, E, GM, MT, QK, CT, X_, XT, PP, VB, KG, QD, R2 = gd_t
            dve.wait_ge(gd["ab_hi"], 1)
            tt(ab_lo[:], ab_raw[:], ab_hi[:].bitcast(F32), ALU.subtract, gd["ab_lo"])
            dve.wait_ge(taken[0], USES["out"][0])
            per_head = [P, NT, HEADS]
            v.tensor_scalar(beta, ab[:, :, HEADS:], LOWEST, None, ALU.max).then_inc(gd["bf"], 1)
            st.link(tt(gs_t1, ab[:, :, 0:HEADS], dt_b.unsqueeze(1).to_broadcast(per_head), ALU.add))
            v.scalar_tensor_tensor(out=gs_t2, in0=gs_t1, scalar=-1.0, in1=gs_t1, op0=ALU.mult, op1=ALU.max).then_inc(gd["z"], 1)
            dve.wait_ge(gd["eb"], 1)
            sigmoid_tail(beta)
            dve.wait_ge(gd["lz"], 1)
            dve.wait_ge(gd["ea"], 1)
            st.link(v.scalar_tensor_tensor(out=gs_t1, in0=gs_t1, scalar=0.0, in1=gs_t2, op0=ALU.max, op1=ALU.add))
            v.scalar_tensor_tensor(out=log_a, in0=gs_t1, scalar=-1.0, in1=a_log.unsqueeze(1).to_broadcast(per_head),
                                   op0=ALU.mult, op1=ALU.mult).then_inc(gd["la"], 1)
            n = TILE[("gs", 0, "g")]
            take(n)
            v.tensor_copy(g_cum, flat(n)[:, 0:NT * HEADS].rearrange("p (t n) -> p t n", t=NT)).then_inc(gd["g"], 1)
            dve.wait_ge(gd["eg"], 1)
            st.link(tt(bg, bg, beta, ALU.mult))
            for g in range(GROUPS):
                def T(name):
                    return TILE[("gdn", g, name)]

                def W(name, k=1, n=1):
                    dve.wait_ge(gd[name], g * n + k)

                def heads_of(x, t=None):
                    r = x[:, :, g * GH:(g + 1) * GH].rearrange("p t j -> p j t")
                    return r if t is None else r[:, :, t]

                def over4(x):
                    return heads_of(x).unsqueeze(3).to_broadcast([P, GH, NT, P])

                def jt(x):
                    return x.rearrange("p (j t) n -> p j t n", t=NT)

                def psum(name):
                    return flat(T(name)).rearrange("p (u n) -> p u n", n=P)

                taps = col("gdn_conv")
                for x, (name, c) in enumerate((("q", QF), ("k", KF), ("v", VF))):
                    take(T(name))
                    src, dst = flat(T(name)).rearrange("p (j n) -> p j n", j=GH), tile(c).rearrange("p (j n) -> p j n", j=GH)
                    for tap in (3, 2, 1, 0):
                        back = 3 - tap
                        for j in range(GH):
                            w = taps[:, 24 * tap + HEADS * x + g * GH + j:24 * tap + HEADS * x + g * GH + j + 1]
                            if back == 0:
                                ins = v.tensor_scalar(dst[:, j], src[:, j], w, None, ALU.mult)
                            else:
                                ins = v.scalar_tensor_tensor(out=dst[:, j, back:], in0=src[:, j, :SEQ - back], scalar=w,
                                                             in1=dst[:, j, back:], op0=ALU.mult, op1=ALU.add)
                        if tap:
                            st.link(ins)
                    ins.then_inc(gd["conv"], 1)
                for x, (c, e) in enumerate(((QF, CT), (KF, X_), (VF, XT))):
                    W("ce", x + 1, 3)
                    sigmoid_tail(tile(e))
                    tt(tile(c), tile(c), tile(e), ALU.mult, gd["silu"])
                W("silu", 3, 3)
                v.tensor_copy(jt(XT), over4(log_a)).then_inc(gd["lab"], 1)
                v.tensor_copy(jt(PP), over4(beta)).then_inc(gd["bb"], 1)
                W("ln", 1, 2)
                v.scalar_tensor_tensor(out=tile(QF), in0=tile(QF), scalar=float(P) ** -0.5, in1=tile(CT),
                                       op0=ALU.mult, op1=ALU.mult)
                W("ln", 2, 2)
                st.link(tt(tile(KF), tile(KF), tile(X_), ALU.mult))
                take(T("beta"))
                tt(QD[:], KF[:], psum("beta"), ALU.mult, gd["kb"])
                W("gc")
                st.link(tt(jt(GM), jt(VB), over4(g_cum), ALU.subtract))
                v.tensor_scalar(tile(GM), tile(GM), 0.0, None, ALU.min).then_inc(gd["d"], 1)
                tt(ktl, jt(VB)[:, :, 0, P - 1], heads_of(g_cum, 0), ALU.subtract, gd["ke"])
                W("ge")
                st.link(tt(GM[:], GM[:], upper.unsqueeze(1).to_broadcast([P, UN, P]), ALU.mult))
                take(T("kk"))
                tt(MT[:], psum("kk"), GM[:], ALU.mult, gd["kk"])
                take(T("qk"))
                tt(QK[:], psum("qk"), GM[:], ALU.mult, gd["qk"])
                take(T("kt"))
                W("ktl")
                tt(KG[:, 0:GH], jt(psum("kt"))[:, :, 1], heads_of(bg, 1).unsqueeze(2).to_broadcast([P, GH, P]), ALU.mult)
                tt(KG[:, GH:UN], jt(psum("kt"))[:, :, 0], over(ktl, GH), ALU.mult, gd["kg"])
                take(T("vt"))
                W("qde")
                tt(jt(VB), jt(psum("vt")), over4(beta), ALU.mult, gd["vb"])
                tt(QD[:, 0:GH], jt(QF)[:, :, 1], QD[:, GH:UN], ALU.mult, gd["qd"])

                def joined(lev):
                    tt([CT, VF][lev % 2][:], MT[:], level(lev).unsqueeze(1).to_broadcast([P, UN, P]), ALU.mult, gd["ct"])

                joined(0)
                joined(1)
                eye = ident.unsqueeze(1).to_broadcast([P, UN, P])
                W("ct", 1, LEVELS)
                take(T("p0"))
                tt(XT[:], eye, CT[:], ALU.subtract)
                tt(X_[:], eye, psum("p0"), ALU.subtract, gd["x"])
                for lev in range(1, LEVELS):
                    if lev + 1 < LEVELS:
                        W("x", lev, LEVELS)
                        joined(lev + 1)
                    if lev < LEVELS - 1:
                        take(T(f"xp{lev}"))
                        tt(X_[:], X_[:], psum(f"xp{lev}"), ALU.subtract, gd["xx"])
                    take(T(f"px{lev}"))
                    tt(XT[:], XT[:], psum(f"px{lev}"), ALU.subtract, gd["x"])
                gate_finish(gd, g, R2)
                take(T("ws"))
                W("u")
                tt(jt(PP)[:, :, 1], jt(PP)[:, :, 1], flat(T("ws"))[:, 0:GH * P].rearrange("p (j n) -> p j n", n=P),
                   ALU.subtract, gd["vn"])
                finish_heads(gd, g, T, XT, "osq", X_, R2, op_b[1], 8)

            def lows(g, n, hooks):
                for k in range(n):
                    split_lo(dve, g, k, k)
                    if k in hooks:
                        hooks[k]()

            with dve.Fori(0, 4) as c:
                lows(GEMM["out"] + KP * c, KP, {})
            dve.wait_ge(late, 64)
            for q in range(2):
                for h in range(2):
                    n = TILE[("gt", 0, "mf"[q] + str(h))]
                    take(n)
                    part = slice(1024 * h, 1024 * (h + 1))
                    tt(acc[:, q, part], flat(n), gate_rows[:, 2 * q, part], ALU.add, gt_ready)
                    dve.wait_ge(gt_ready, 2 * q + h + 1)
                    st.link(tt(acc[:, q, part], acc[:, q, part], gate_rows[:, 2 * q + 1, part], ALU.mult))

            def residual(r, q):
                newton(r)
                for t in range(NT):
                    st.link(v.scalar_tensor_tensor(out=Y[:, t], in0=Y[:, t], scalar=r_n[:, t:t + 1], in1=acc[:, q],
                                                   op0=ALU.mult, op1=ALU.mult))
                st.link(tt(X[:], X[:], Y[:], ALU.add))
                v.tensor_copy(r_b, r_n).then_inc(norm_src, 1)

            dve.wait_ge(x_landed, 32)
            residual(1, 0)
            operand("op1", 1, 2, scale_f, shift_f)

            def add_down(dst, i, c, g):
                x = (c + 1) % 2
                dve.wait_ge(w_used, g)
                tt(dst[:, :, CH * c:CH * (c + 1)], dst[:, :, CH * c:CH * (c + 1)], pair(x), ALU.add, taken[x])

            def low_hidden(i):
                dve.wait_ge(ff["hi"], i + 1)
                tt(hid[1][:].rearrange("p k n -> p (k n)"), flat(0), hid[0][:].rearrange("p k n -> p (k n)").bitcast(F32),
                   ALU.subtract, ff["lo"])

            s0, g0 = STREAM["ffn"], GEMM["ffn"]
            lows(g0, KP, {})
            dve.wait_ge(ff["zero"], 1)

            def ffn_turn(i, first=False):
                g = g0 - 8 + 16 * i
                hooks = {5: lambda: low_hidden(i - 1), 13: lambda: add_down(Y, i, 0, g + 10),
                         15: lambda: add_down(Y, i, 1, g + 12)}
                if not first:
                    hooks[1] = lambda: add_down(Y, i, 2, g - 2)
                    hooks[3] = lambda: add_down(Y, i, 3, g)
                lows(g, 16, hooks)

            ffn_turn(1, True)
            with dve.Fori(2, FF1 // CH) as i:
                ffn_turn(i)
            i, g = FF1 // CH - 1, g0 + 248
            lows(g, 8, {1: lambda: add_down(Y, i, 2, g - 2), 2: lambda: (add_down(Y, i, 3, g), low_hidden(i)),
                        5: lambda: add_down(Y, i, 0, g + 2), 7: lambda: add_down(Y, i, 1, g + 4)})
            add_down(Y, i, 2, g + 6)
            add_down(Y, i, 3, g + 8)
            residual(3, 1)
            operand("op2", 2, 4, col("mix2"), None)

            with dve.Fori(0, 9) as c:
                lows(GEMM["in2"] + KP * c, KP, {})
            C, M = at_t[0], at_t[1]
            taps_a = col("conv_a")
            for g in range(2):
                n = TILE[("att", 0, f"cv{g}")]
                take(n)
                src, dst = flat(n).rearrange("p (j n) -> p j n", j=4), tile(C).rearrange("p (j n) -> p j n", j=4)

                def w(tap, j):
                    return taps_a[:, 8 * tap + 4 * g + j:8 * tap + 4 * g + j + 1]

                for j in range(4):
                    ins = v.tensor_scalar(dst[:, j], src[:, j], w(1, j), None, ALU.mult)
                st.link(ins)
                for j in range(4):
                    ins = v.scalar_tensor_tensor(out=dst[:, j, 1:], in0=src[:, j, :SEQ - 1], scalar=w(0, j), in1=dst[:, j, 1:],
                                                 op0=ALU.mult, op1=ALU.add)
                st.link(ins)
                for j in range(4):
                    ins = v.scalar_tensor_tensor(out=dst[:, j, :SEQ - 1], in0=src[:, j, 1:], scalar=w(2, j),
                                                 in1=dst[:, j, :SEQ - 1], op0=ALU.mult, op1=ALU.add)
                ins.then_inc(att["conv"], 1)
                dve.wait_ge(att["conv"], g + 1)
                n = TILE[("att", 0, f"b{g}")]
                take(n)
                tt(tile(M), tile(C), flat(n), ALU.mult, att["m"])
                dve.wait_ge(att["hi"], g + 1)
                part = [op_b[0][x][:, 4 * g:4 * g + 4].rearrange("p k n -> p (k n)") for x in range(2)]
                tt(part[1], tile(M), part[0].bitcast(F32), ALU.subtract, att["lo"])

            S, KR, TMP = at_t[0:2], at_t[2], at_t[3]

            def rotate(t, src, heads, outs, s=None):
                cos = table[:, C_COS + 32 * t:C_COS + 32 * (t + 1)].unsqueeze(1).to_broadcast([P, heads, 32])
                sin = table[:, C_SIN + 32 * t:C_SIN + 32 * (t + 1)].unsqueeze(1).to_broadcast([P, heads, 32])
                t1 = tile(TMP)[:, 0:heads * 32].rearrange("p (h n) -> p h n", n=32)
                t2 = tile(TMP)[:, 512:512 + heads * 32].rearrange("p (h n) -> p h n", n=32)
                x1, x2 = src[:, :, 0:32], src[:, :, 32:64]
                tt(t1, x1, cos, ALU.mult)
                st.link(tt(t2, x2, sin, ALU.mult))
                for o in outs:
                    ins = tt(o[:, :, 0:32], t1, t2, ALU.subtract)
                st.link(ins)
                tt(t1, x2, cos, ALU.mult)
                st.link(tt(t2, x1, sin, ALU.mult))
                for o in outs:
                    ins = tt(o[:, :, 32:64], t1, t2, ALU.add)
                if s is None:
                    st.link(ins)
                else:
                    ins.then_inc(s, 1)

            for t in range(NT):
                src = proj2[:, t, 8 * CH:8 * CH + AKV * AD].rearrange("p (h n) -> p h n", n=AD)
                kr = KR[:, 4 * t:4 * t + 4]
                rotate(t, src, AKV, [kr[:, :, 0:AD], kr[:, :, AD:2 * AD]], att["kr"] if t else None)
            dve.wait_ge(att["kr"], 1)
            for t in range(NT):
                src = proj2[:, t, 6 * CH:8 * CH].rearrange("p (h n) -> p h n", n=AD)
                rotate(t, src, AH, [tile(S[t]).rearrange("p (h n) -> p h n", n=AD)], att["qr"] if t else None)

            def soft(b):
                kv, t, o = b // 2, b % 2, 4 * (b % 2)
                n = TILE[("att", 0, f"sc{b}")]
                take(n)
                sc = tile(S[b % 2]).rearrange("p (u n) -> p u n", n=SEQ)
                mask = table[:, C_MASK + SEQ * t:C_MASK + SEQ * (t + 1)].unsqueeze(1).to_broadcast([P, 4, SEQ])
                v.scalar_tensor_tensor(out=sc, in0=flat(n).rearrange("p (u n) -> p u n", n=SEQ), scalar=AD ** -0.5, in1=mask,
                                       op0=ALU.mult, op1=ALU.add).then_inc(att["s"], 1)
                dve.wait_ge(att["s"], b + 1)
                if b >= 2:
                    dve.wait_ge(att["es"], b - 1)
                st.link(v.tensor_reduce(k_mx[:, o:o + 4], sc, AX.X, ALU.max))
                snk = sink[:, 4 * kv:4 * kv + 4].rearrange("p (x r) -> p r x", r=2)
                mx = k_mx[:, o:o + 4].rearrange("p (r x) -> p r x", r=2)
                st.link(tt(mx, mx, snk, ALU.max))
                tt(k_es[:, o:o + 4].rearrange("p (r x) -> p r x", r=2), snk, mx, ALU.subtract)
                v.tensor_scalar(k_nm[:, o:o + 4], k_mx[:, o:o + 4], -1.0, None, ALU.mult).then_inc(att["mx"], 1)

            def weigh(b):
                kv, t, o = b // 2, b % 2, 4 * (b % 2)
                dve.wait_ge(att["es"], b + 1)
                st.link(tt(k_rd[:, o:o + 4], k_sum[:, o:o + 4], k_es[:, o:o + 4], ALU.add))
                st.link(v.reciprocal(k_rd[:, o:o + 4], k_rd[:, o:o + 4]))
                n = TILE[("att", 0, f"pv{b}")]
                take(n)
                c0 = 6 * CH + 4 * kv * AD
                dst = proj2[:, t, c0:c0 + 4 * AD].rearrange("p (x r d) -> p r x d", r=2, d=AD)
                src = flat(n)[:, 0:4 * AD].rearrange("p (r x d) -> p r x d", r=2, d=AD)
                rd = k_rd[:, o:o + 4].rearrange("p (r x) -> p r x", r=2).unsqueeze(3).to_broadcast([P, 2, 2, AD])
                tt(dst, src, rd, ALU.mult, att["pv"])

            soft(0)
            for b in range(8):
                if b < 7:
                    soft(b + 1)
                weigh(b)
            for x in range(2):
                dve.wait_ge(att["hi"], 3 + x)
                part = [op_b[1][y][:, 4 * x:4 * x + 4].rearrange("p k n -> p (k n)") for y in range(2)]
                tt(part[1], flat(TILE[("att", 0, f"at{x}")]), part[0].bitcast(F32), ALU.subtract, att["lo"])

            g0, u = GEMM["gate"], USES["gate"]
            dve.wait_ge(gate["rows"], 32)

            def gate_in(n, x, z, g):
                dve.wait_ge(w_used, g)
                if isinstance(n, int):
                    b = gbias[:, x, CH * n:CH * (n + 1)].unsqueeze(1)
                else:
                    b = gbias[:, x:x + 1, bass.ds(CH * n, CH)]
                tt(z[:], pair(x), b.to_broadcast([P, NT, CH]), ALU.add, taken[x])
                dve.wait_ge(taken[x], u[x] + 2 * n + 1)
                v.tensor_scalar(z[:], z[:], LOWEST, None, ALU.max).then_inc(gate["z"], 1)

            def gate_out(n, x, z):
                dve.wait_ge(gate["e"], 2 * n + x + 1)
                v.tensor_scalar(z[:], z[:], 1.0, None, ALU.add).then_inc(gate["r"], 1)
                dve.wait_ge(gate["r"], 4 * n + 2 * x + 1)
                v.reciprocal(z[:], z[:]).then_inc(gate["r"], 1)

            def branch(n, x, z, g):
                dve.wait_ge(w_used, g)
                dve.wait_ge(gate["r"], 4 * n + 2 * x + 2)
                dve.wait_ge(gate["made"], n)
                tt(ma[:, x], pair(x), z[:], ALU.mult, taken[x])

            def low_mixed(n):
                dve.wait_ge(gate["hi"], n + 1)
                r = [op_c[y][:, bass.ds(4 * n, 4)].rearrange("p k n -> p (k n)") for y in range(2)]
                tt(r[1], flat(0), r[0].bitcast(F32), ALU.subtract, gate["lo"])

            def gate_turn(n, first=False):
                g = g0 + 24 * n
                hooks = {10: lambda: gate_in(n, 0, za, g + 8), 14: lambda: gate_out(n, 0, za),
                         18: lambda: gate_in(n, 1, zb, g + 16), 22: lambda: (gate_out(n, 1, zb), branch(n, 0, za, g + 20))}
                if not first:
                    hooks[2] = lambda: branch(n - 1, 1, zb, g)
                    hooks[13] = lambda: low_mixed(n - 1)
                lows(g, 24, hooks)

            gate_turn(0, True)
            with dve.Fori(1, 4) as n:
                gate_turn(n)
            branch(3, 1, zb, g0 + 96)
            low_mixed(3)

            g0 = GEMM["mix"]

            def add_mix(n, x, g):
                dve.wait_ge(w_used, g)
                d = X[:, :, bass.ds(CH * n, CH)]
                tt(d, d, pair(x), ALU.add, taken[x])

            for n in range(4):
                lows(g0 + KP * n, KP, {2: lambda: add_mix(n - 1, (n - 1) % 2, g0 + KP * n)} if n else {})
            add_mix(3, 1, g0 + KP * 4)
            operand("op3", 3, 5, col("ffn2"), None)

            g0 = GEMM["ffn2"]
            taps_f, bias_f = [cols[:, 2 + k, 0:88] for k in range(3)], col("ffn_bias")

            def conv_up(i, k, dst, s):
                dve.wait_ge(f2["made"], 2 * i + k + 1)
                c0 = 44 * k + 4 * i

                def at_(t_, j):
                    return t_[:, c0 + j:c0 + j + 1] if isinstance(i, int) else t_[:, bass.ds(c0 + j, 1)]

                src = flat(0).rearrange("p (j n) -> p j n", j=4)
                for j in range(4):
                    ins = v.tensor_scalar(dst[:, j], src[:, j], at_(taps_f[1], j), at_(bias_f, j), ALU.mult, ALU.add)
                ins.then_inc(f2["sum"], 1)
                dve.wait_ge(f2["sum"], 4 * i + 2 * k + 1)
                for j in range(4):
                    ins = v.scalar_tensor_tensor(out=dst[:, j, 1:], in0=src[:, j, :SEQ - 1], scalar=at_(taps_f[0], j),
                                                 in1=dst[:, j, 1:], op0=ALU.mult, op1=ALU.add)
                ins.then_inc(f2["sum"], 1)
                dve.wait_ge(f2["sum"], 4 * i + 2 * k + 2)
                for j in range(4):
                    ins = v.scalar_tensor_tensor(out=dst[:, j, :SEQ - 1], in0=src[:, j, 1:], scalar=at_(taps_f[2], j),
                                                 in1=dst[:, j, :SEQ - 1], op0=ALU.mult, op1=ALU.add)
                ins.then_inc(s, 1)

            def floor_up(i):
                dve.wait_ge(f2["cva"], i + 1)
                if not (isinstance(i, int) and i == 0):
                    dve.wait_ge(f2["lo"], i)
                v.tensor_scalar(sga[:], cva[:], LOWEST, None, ALU.max).then_inc(f2["z"], 1)

            def product_up(i):
                dve.wait_ge(f2["e"], i + 1)
                dve.wait_ge(f2["cvg"], i + 1)
                for k in range(4):
                    if k == 0:
                        ins = v.tensor_scalar(sga[:], sga[:], 1.0, None, ALU.add)
                    elif k == 1:
                        ins = v.reciprocal(sga[:], sga[:])
                    else:
                        ins = tt(sga[:], sga[:], (cva, cvg)[k - 2][:], ALU.mult)
                    if k < 3:
                        ins.then_inc(f2["q"], 1)
                        dve.wait_ge(f2["q"], 3 * i + k + 1)
                ins.then_inc(f2["h"], 1)

            def low_hidden2(i):
                dve.wait_ge(f2["hi"], i + 1)
                tt(hid2[1][:], sga[:], hid2[0][:].bitcast(F32), ALU.subtract, f2["lo"])

            lows(g0, 16, {})
            conv_up(0, 0, cva, f2["cva"])
            floor_up(0)

            def ffn2_turn(i, first=False):
                g = g0 - 8 + 24 * i
                hooks = {5: lambda: product_up(i - 1), 9: lambda: low_hidden2(i - 1),
                         19: lambda: conv_up(i, 0, cva, f2["cva"]),
                         21: lambda: add_down(X, i, 0, g + 18),
                         22: lambda: floor_up(i),
                         23: lambda: (add_down(X, i, 1, g + 20), conv_up(i, 1, cvg, f2["cvg"]))}
                if first:
                    hooks[1] = lambda: conv_up(0, 1, cvg, f2["cvg"])
                else:
                    hooks[1] = lambda: add_down(X, i, 2, g - 2)
                    hooks[3] = lambda: add_down(X, i, 3, g)
                lows(g, 24, hooks)

            ffn2_turn(1, True)
            with dve.Fori(2, FF2 // CH) as i:
                ffn2_turn(i)
            i, g = FF2 // CH - 1, g0 + 256
            lows(g, 8, {1: lambda: add_down(X, i, 2, g - 2),
                        2: lambda: (add_down(X, i, 3, g), product_up(i), low_hidden2(i)),
                        5: lambda: add_down(X, i, 0, g + 2), 7: lambda: add_down(X, i, 1, g + 4)})
            add_down(X, i, 2, g + 6)
            add_down(X, i, 3, g + 8)
            newton(6)
            dve.wait_ge(fin["rows"], 16)
            for t in range(NT):
                v.scalar_tensor_tensor(out=XN[:, t], in0=X[:, t], scalar=r_n[:, t:t + 1], in1=fin_norm[:],
                                       op0=ALU.mult, op1=ALU.mult).then_inc(fin["out"], 1)

        @block.gpsimd
        def _(pool):
            p = nc.gpsimd

            def tile(t):
                return t[:].rearrange("p u n -> p (u n)")

            p.memset(rows[:], 0.0).then_inc(rows_zeroed, 1)
            p.memset(acc[:], 0.0).then_inc(acc_zeroed, 1)
            Q, K, B, D0, D1, QE0, QE1, KE0, KE1, A, R = hg_t
            for t in (QE0, QE1, KE0, KE1, A):
                ins = p.memset(t[:], 0.0)
            ins.then_inc(hg["zero"], 1)
            pool.wait_ge(made, TILE[("mod", 0, "shsc")] + 1)
            p.memset(acc[:], 0.0).then_inc(acc_zeroed, 1)

            def gate_floor(s, g, R_):
                src = proj[:, :, 3072 + g * GH * P:3072 + (g + 1) * GH * P].rearrange("p t (j n) -> p j t n", n=P)
                p.tensor_scalar(R_[:].rearrange("p (j t) n -> p j t n", t=NT), src, LOWEST, None, ALU.max) \
                    .then_inc(s["gf"], 1)

            def gate_mul(s, g, R_, which):
                pool.wait_ge(s["gr"], g + 1)
                src = proj[:, :, 3072 + g * GH * P:3072 + (g + 1) * GH * P].rearrange("p t (j n) -> p j t n", n=P)
                dst = R_[:].rearrange("p (j t) n -> p j t n", t=NT)
                p.tensor_tensor(dst, dst, src, ALU.mult).then_inc(pool_step, 1)
                steps[0] += 1
                pool.wait_ge(pool_step, steps[0])
                p.tensor_tensor(R_[:], R_[:], head_norm[:, which].unsqueeze(1).to_broadcast([P, UN, P]),
                                ALU.mult).then_inc(s["gate"], 1)

            steps = [0]
            DD, KE = [D0, D1], [KE0, KE1]
            pool.wait_ge(taken[0], USES["gdn"][0])
            pool.wait_ge(taken[1], USES["gdn"][1])
            for g in range(GROUPS):
                if g:
                    pool.wait_ge(hg["o"], g)
                gate_floor(hg, g, R)
                for lev in range(LEVELS):
                    h = 1 << lev

                    def blocks(t):
                        return tile(t).rearrange("p (b n) -> p b n", n=2 * h)[:, :, :h]

                    pool.wait_ge(hg["exp"], LEVELS * g + lev + 1)
                    if lev >= 2:
                        pool.wait_ge(made, TILE[("hg", g, f"lev{lev - 2}")] + 1)
                    p.tensor_tensor(blocks(KE[lev % 2]), blocks(K), blocks(DD[lev % 2]), ALU.mult).then_inc(hg["ke"], 1)
                gate_mul(hg, g, R, 0)
            pool.wait_ge(made, TILE[("mod2", 0, "shsc")] + 1)
            p.memset(acc[:], 0.0).then_inc(acc_zeroed, 1)
            QF, KF, VF, E, GM, MT, QK, CT, X_, XT, PP, VB, KG, QD, R2 = gd_t
            pool.wait_ge(gd["ab"], 1)
            pool.wait_ge(taken[1], USES["out"][1])
            for g in range(GROUPS):
                if g:
                    pool.wait_ge(gd["o"], g)
                gate_floor(gd, g, R2)
                for x, (c, e) in enumerate(((QF, CT), (KF, X_), (VF, XT))):
                    pool.wait_ge(gd["conv"], 3 * g + x + 1)
                    p.tensor_scalar(tile(e), tile(c), LOWEST, None, ALU.max).then_inc(gd["cf"], 1)
                gate_mul(gd, g, R2, 1)
            pool.wait_ge(norm_src, 1)
            p.memset(Y[:], 0.0).then_inc(ff["zero"], 1)
            pool.wait_ge(taken[0], USES["gate"][0])
            pool.wait_ge(taken[1], USES["gate"][1])
            for g in range(2):
                c = proj2[:, :, (2 + g) * CH:(3 + g) * CH]
                p.tensor_tensor(c, c, proj2[:, :, (4 + g) * CH:(5 + g) * CH], ALU.mult).then_inc(att["cv"], 1)
            with pool.Fori(0, 4) as n:
                pool.wait_ge(taken[1], USES["gate"][1] + 2 * n + 2)
                p.tensor_tensor(ma[:, 0], ma[:, 0], ma[:, 1], ALU.add).then_inc(gate["m"], 1)


NAMES = ["x", "c", "w_ada", "b_ada", "pre_mix_norm", "post_mix_norm", "pre_ffn_norm", "post_ffn_norm", "w_in",
         "hg_lb_logits", "hg_norm", "gdn_conv_w", "gdn_a_log", "gdn_dt_bias", "gdn_norm", "w_out", "w_ff1", "w_ff2",
         "norm_mix_g_2", "w_in_2", "b_gate_2", "conv_a_w_2", "w_out_a_2", "sink_logits_2", "w_o_attn_2",
         "w_mix_out_2", "norm_ffn_g_2", "ffn_w_up_2", "ffn_conv_w_2", "ffn_conv_b_2", "ffn_w_down_2", "norm_final_g_2"]


def kernel(**inputs):
    import concourse.bacc as bacc
    from concourse.bass_utils import run_bass_kernel_spmd

    nc = bacc.Bacc("TRN2", target_bir_lowering=False, num_devices=1)
    arrays, ins = {}, {}
    for name in NAMES:
        x = np.ascontiguousarray(inputs[name])
        arrays[f"in_{name}"] = x
        ins[name] = nc.dram_tensor(f"in_{name}", x.shape, mybir.dt.from_np(x.dtype), kind="ExternalInput").ap()
    arrays["constants"] = constants()
    consts = nc.dram_tensor("constants", (P, C_END), F32, kind="ExternalInput").ap()
    out = nc.dram_tensor("out", (1, SEQ, D), F32, kind="ExternalOutput").ap()
    two_blocks(nc, ins, consts, out)
    r = run_bass_kernel_spmd(nc, [arrays], core_ids=[0])
    return r.results[0]["out"]
```
